# Optimizing a Trainium2 kernel written in Bass

```python
import math
import jax, jax.numpy as jnp
from jax import lax
import numpy as np

D_MODEL = 1024
BATCH = 1
SEQ = 512
DEPTH = 2

CHUNK = 64
N_MIXERS = 2
N_A = (DEPTH + 1) // 2
N_B = DEPTH // 2
N_HEADS_A = 16
HEAD_DIM_A = D_MODEL // N_HEADS_A
Q_BLOCK = 128
D_RNN = D_MODEL
N_BLOCKS_B = 8
BLOCK_B = D_RNN // N_BLOCKS_B
CONV_B = 4
LRU_C = 8.0
D_FF = 2816
CONV_F = 3
D_PLE = 256
LN_EPS = 1e-5
ALPHA = (2.0 * DEPTH) ** 0.25
BETA = (8.0 * DEPTH) ** -0.25

kernel_name = "fox_rglru_deepnorm_convffn_hybrid"

def layer_norm(x, g, b):
    xf = x.astype(jnp.float32)
    mu = jnp.mean(xf, axis=-1, keepdims=True)
    xc = xf - mu
    var = jnp.mean(xc * xc, axis=-1, keepdims=True)
    y = xc * lax.rsqrt(var + LN_EPS) * g.astype(jnp.float32) + b.astype(jnp.float32)
    return y.astype(x.dtype)

def causal_dwconv(x, w, b):
    k, c = w.shape
    y = lax.conv_general_dilated(
        x, w[:, None, :].astype(x.dtype), window_strides=(1,), padding=[(k - 1, 0)],
        dimension_numbers=("NWC", "WIO", "NWC"), feature_group_count=c)
    return y + b.astype(x.dtype)

def forgetting_attention(x, w_in, b_f, w_out):
    bsz, s, _ = x.shape
    h, dh = N_HEADS_A, HEAD_DIM_A
    proj = x @ w_in
    q, k, v, fg = jnp.split(proj, [D_MODEL, 2 * D_MODEL, 3 * D_MODEL], axis=-1)
    q = q.reshape(bsz, s, h, dh).transpose(0, 2, 1, 3)
    k = k.reshape(bsz, s, h, dh).transpose(0, 2, 1, 3)
    v = v.reshape(bsz, s, h, dh).transpose(0, 2, 1, 3)
    log_f = jax.nn.log_sigmoid((fg + b_f).astype(jnp.float32))
    c = jnp.cumsum(log_f, axis=1).transpose(0, 2, 1)
    n_blk = s // Q_BLOCK
    qb = q.reshape(bsz, h, n_blk, Q_BLOCK, dh).transpose(2, 0, 1, 3, 4)
    cb = c.reshape(bsz, h, n_blk, Q_BLOCK).transpose(2, 0, 1, 3)
    pos_k = jnp.arange(s)
    scale = 1.0 / math.sqrt(dh)

    def one_block(args):
        q_i, c_i, i = args
        logits = jnp.einsum("bhqd,bhkd->bhqk", q_i, k).astype(jnp.float32) * scale
        logits = logits + c_i[..., None] - c[:, :, None, :]
        pos_q = i * Q_BLOCK + jnp.arange(Q_BLOCK)
        mask = pos_k[None, :] <= pos_q[:, None]
        logits = jnp.where(mask, logits, -jnp.inf)
        probs = jax.nn.softmax(logits, axis=-1)
        return jnp.einsum("bhqk,bhkd->bhqd", probs.astype(v.dtype), v)

    o = lax.map(one_block, (qb, cb, jnp.arange(n_blk)))
    o = o.transpose(1, 0, 3, 2, 4).reshape(bsz, s, D_MODEL)
    return o @ w_out

def rglru_block(x, w_in, conv_w, conv_b, w_a, b_a, w_i, b_i, lam, w_out):
    bsz, s, _ = x.shape
    proj = x @ w_in
    xb, gb = jnp.split(proj, [D_RNN], axis=-1)
    xb = causal_dwconv(xb, conv_w, conv_b)
    xh = xb.reshape(bsz, s, N_BLOCKS_B, BLOCK_B)
    r = jax.nn.sigmoid(jnp.einsum("bsnc,ncd->bsnd", xh, w_a) + b_a).reshape(bsz, s, D_RNN)
    ig = jax.nn.sigmoid(jnp.einsum("bsnc,ncd->bsnd", xh, w_i) + b_i).reshape(bsz, s, D_RNN)
    log_a = -LRU_C * r.astype(jnp.float32) * jax.nn.softplus(-lam.astype(jnp.float32))
    a = jnp.exp(log_a)
    mult = jnp.sqrt(-jnp.expm1(2.0 * log_a))
    u = mult * (ig * xb).astype(jnp.float32)

    def combine(left, right):
        a1, b1 = left
        a2, b2 = right
        return a1 * a2, a2 * b1 + b2

    _, hseq = lax.associative_scan(combine, (a, u), axis=1)
    y = hseq.astype(x.dtype) * jax.nn.gelu(gb)
    return y @ w_out

def conv_ffn(x, w_up, conv_w, conv_b, w_down):
    hdn = x @ w_up
    hdn = causal_dwconv(hdn, conv_w, conv_b)
    val, gate = jnp.split(hdn, [D_FF], axis=-1)
    return (jax.nn.gelu(gate) * val) @ w_down

def setup_inputs(seed: int = 0) -> dict:
    key = jax.random.key(seed)
    ks = jax.random.split(key, 32)
    f32 = jnp.float32
    nrm = lambda k, shape, sc: jax.random.normal(k, shape, f32) * sc
    x = nrm(ks[0], (BATCH, SEQ, D_MODEL), 1.0)
    p = nrm(ks[1], (DEPTH, BATCH, SEQ, D_PLE), 1.0)
    col_scale = jnp.concatenate([
        jnp.ones((2 * D_MODEL,), f32),
        jnp.full((D_MODEL,), BETA, f32),
        jnp.full((N_HEADS_A,), 0.1, f32)])
    a_w_in = nrm(ks[2], (N_A, D_MODEL, 3 * D_MODEL + N_HEADS_A), D_MODEL ** -0.5) * col_scale
    a_b_f = jnp.linspace(1.0, 6.0, N_HEADS_A, dtype=f32)[None, :] + nrm(ks[3], (N_A, N_HEADS_A), 0.1)
    a_w_out = nrm(ks[4], (N_A, D_MODEL, D_MODEL), D_MODEL ** -0.5 * BETA)
    b_w_in = nrm(ks[5], (N_B, D_MODEL, 2 * D_RNN), D_MODEL ** -0.5)
    b_conv_w = nrm(ks[6], (N_B, CONV_B, D_RNN), CONV_B ** -0.5)
    b_conv_b = nrm(ks[7], (N_B, D_RNN), 0.02)
    b_w_a = nrm(ks[8], (N_B, N_BLOCKS_B, BLOCK_B, BLOCK_B), BLOCK_B ** -0.5)
    b_b_a = nrm(ks[9], (N_B, N_BLOCKS_B, BLOCK_B), 0.02)
    b_w_i = nrm(ks[10], (N_B, N_BLOCKS_B, BLOCK_B, BLOCK_B), BLOCK_B ** -0.5)
    b_b_i = nrm(ks[11], (N_B, N_BLOCKS_B, BLOCK_B), 0.02)
    a_pow_c = jax.random.uniform(ks[12], (N_B, D_RNN), f32, 0.9, 0.999)
    a_base = a_pow_c ** (1.0 / LRU_C)
    b_lam = jnp.log(a_base) - jnp.log1p(-a_base)
    b_w_out = nrm(ks[13], (N_B, D_RNN, D_MODEL), D_RNN ** -0.5 * BETA)
    f_w_up = nrm(ks[14], (DEPTH, D_MODEL, 2 * D_FF), D_MODEL ** -0.5)
    f_conv_w = nrm(ks[15], (DEPTH, CONV_F, 2 * D_FF), CONV_F ** -0.5)
    f_conv_b = nrm(ks[16], (DEPTH, 2 * D_FF), 0.02)
    f_w_down = nrm(ks[17], (DEPTH, D_FF, D_MODEL), D_FF ** -0.5 * BETA)
    ln1_g = 1.0 + nrm(ks[18], (DEPTH, D_MODEL), 0.02)
    ln1_b = nrm(ks[19], (DEPTH, D_MODEL), 0.02)
    ln2_g = 1.0 + nrm(ks[20], (DEPTH, D_MODEL), 0.02)
    ln2_b = nrm(ks[21], (DEPTH, D_MODEL), 0.02)
    ple_w = nrm(ks[22], (DEPTH, D_PLE, D_MODEL), D_PLE ** -0.5 * BETA)
    ple_gate_w = nrm(ks[23], (DEPTH, D_MODEL, D_MODEL), D_MODEL ** -0.5)
    ple_gate_b = nrm(ks[24], (DEPTH, D_MODEL), 0.02)
    return {"x": x, "p": p,
            "a_w_in": a_w_in, "a_b_f": a_b_f, "a_w_out": a_w_out,
            "b_w_in": b_w_in, "b_conv_w": b_conv_w, "b_conv_b": b_conv_b,
            "b_w_a": b_w_a, "b_b_a": b_b_a, "b_w_i": b_w_i, "b_b_i": b_b_i,
            "b_lam": b_lam, "b_w_out": b_w_out,
            "f_w_up": f_w_up, "f_conv_w": f_conv_w, "f_conv_b": f_conv_b, "f_w_down": f_w_down,
            "ln1_g": ln1_g, "ln1_b": ln1_b, "ln2_g": ln2_g, "ln2_b": ln2_b,
            "ple_w": ple_w, "ple_gate_w": ple_gate_w, "ple_gate_b": ple_gate_b}

def reference(x, p, a_w_in, a_b_f, a_w_out,
              b_w_in, b_conv_w, b_conv_b, b_w_a, b_b_a, b_w_i, b_b_i, b_lam, b_w_out,
              f_w_up, f_conv_w, f_conv_b, f_w_down,
              ln1_g, ln1_b, ln2_g, ln2_b,
              ple_w, ple_gate_w, ple_gate_b):
    for i in range(DEPTH):
        j = i // N_MIXERS
        if i % N_MIXERS == 0:
            m = forgetting_attention(x, a_w_in[j], a_b_f[j], a_w_out[j])
        else:
            m = rglru_block(x, b_w_in[j], b_conv_w[j], b_conv_b[j], b_w_a[j], b_b_a[j],
                            b_w_i[j], b_b_i[j], b_lam[j], b_w_out[j])
        x = layer_norm(ALPHA * x + m, ln1_g[i], ln1_b[i])
        ff = conv_ffn(x, f_w_up[i], f_conv_w[i], f_conv_b[i], f_w_down[i])
        x = layer_norm(ALPHA * x + ff, ln2_g[i], ln2_b[i])
        gate = jax.nn.sigmoid(x @ ple_gate_w[i] + ple_gate_b[i])
        x = x + gate * (p[i] @ ple_w[i])
    return x


_drawn_inputs = setup_inputs


def setup_inputs(seed=0):
    import zlib

    import numpy as np

    out = dict(_drawn_inputs(seed))
    spreads = {}
    factors = {'b_conv_b': 2.724, 'b_b_a': 64.0, 'b_b_i': 52.981, 'f_conv_b': 6.27, 'ple_gate_b': 8.0}
    for name, (base, spread) in spreads.items():
        noise = np.random.default_rng([zlib.crc32(name.encode()), seed]).standard_normal(out[name].shape)
        drawn = base * np.exp(spread * noise) if base else spread * noise
        out[name] = __import__('jax').numpy.asarray(drawn.astype(out[name].dtype))
    for name, factor in factors.items():
        out[name] = (out[name] * factor).astype(out[name].dtype)
    return out
```

```python
from contextlib import ExitStack

import concourse.bass as bass
from concourse import mybir

F32 = mybir.dt.float32
F32R = mybir.dt.float32r
BF16 = mybir.dt.bfloat16
ALU = mybir.AluOpType
ACT = mybir.ActivationFunctionType
AX_X = mybir.AxisListType.X

P = 128
SEQ = 512
D_MODEL = 1024
DEPTH = 2
HEADS = 16
HEAD_DIM = D_MODEL // HEADS
D_FF = 2816
D_PLE = 256
CONV_F = 3
CONV_B = 4
LN_EPS = 1e-5
ALPHA = (2.0 * DEPTH) ** 0.25
KT = D_MODEL // P
FT = D_FF // P
PAIRS = HEADS // 2
QT = SEQ // P
UNIT = KT * P
SLOTS = 4
LEAD = 3
MASKED = -3.0e38
LOG1P_TERMS = [1.0 / (2 * n + 1) for n in range(9)]

COLS = {}


def _columns():
    at = 0
    for layer in range(DEPTH):
        for name, n in (("ln1_g", KT), ("ln1_b", KT), ("ln2_g", KT), ("ln2_b", KT), ("gate_b", KT),
                        ("conv", 2 * FT * (CONV_F + 1))):
            COLS[name, layer] = at
            at += n
    for name, n in (("rg_conv", KT * (CONV_B + 1)), ("rg_ba", KT), ("rg_bi", KT), ("rg_lam", KT)):
        COLS[name] = at
        at += n
    return at


N_COLS = _columns()


class Phase:

    def __init__(self, name, slots, iters, width, first, used):
        self.name, self.slots, self.iters, self.widths = name, slots, iters, width
        self.first = first
        self.before = list(used)
        self.per_round = [slots.count(s) for s in range(SLOTS)]

    def unit(self, i, r):
        return i * len(self.slots) + (self.first + r)

    def uses(self, i, r):
        s = self.slots[r]
        return i * self.per_round[s] + (self.before[s] + self.slots[:r + 1].count(s))


def plan():
    whole = [UNIT]
    down = [8 * P, 7 * P, 7 * P]
    want = [("qkv", [0, 1, 2], PAIRS, whole), ("out0", [0, 1, 2, 3], 2, whole),
            ("up0", [0, 1, 2, 3], 2 * FT // 4, whole), ("down0", [0, 1, 2] * 2, KT // 2, down),
            ("ple0", [0, 1], 1, whole), ("gate0", [2, 3, 0, 1], 2, whole),
            ("rg", [2, 3, 0, 1], 2 * KT // 4, whole), ("out1", [2, 3, 0, 1], 2, whole),
            ("up1", [2, 3, 0, 1], 2 * FT // 4, whole), ("down1", [2, 3, 0] * 2, KT // 2, down),
            ("ple1", [2, 3], 1, whole), ("gate1", [0, 1, 2, 3], 2, whole)]
    phases, first, used, last = {}, 0, [0] * SLOTS, {}
    for name, slots, iters, widths in want:
        widths = (widths * len(slots))[:len(slots)]
        phases[name] = Phase(name, slots, iters, widths, first, used)
        for i in range(iters):
            for s in slots:
                assert first - last.get(s, -LEAD) >= LEAD, name
                last[s] = first
                used[s] += 1
                first += 1
    return phases


def hybrid_trunk_kernel(nc, xT, pT, w_square, w_down, w_forget, b_forget, w_lru, columns, outT):
    phases = plan()
    with ExitStack() as ctx:
        def sem(name):
            return ctx.enter_context(nc.semaphore(name))

        start = (nc.sbuf_base + 63) // 64 * 64
        size = 206 * 1024
        ctx.enter_context(nc.sbuf_tensor("arena", [P, size // 4], F32))
        at = [start]

        def place(name, shape, dt, where=None):
            n = 4 if dt != BF16 else 2
            for k in shape[1:]:
                n *= k
            n = (n + 63) // 64 * 64
            where = at if where is None else where
            t = nc.alloc_sbuf_tensor_at(name, shape, dt, offset=where[0])
            where[0] += n
            assert where[0] <= start + size, name
            return t

        x = place("x", [P, KT, SEQ], F32)
        x_hi = place("x_hi", [P, KT, SEQ], F32R)
        x_lo = place("x_lo", [P, KT, SEQ], F32R)
        stage = place("stage", [P, SLOTS, UNIT], F32)
        w_hi = place("w_hi", [P, SLOTS, UNIT], F32R)
        w_lo = place("w_lo", [P, SLOTS, UNIT], F32R)
        cols = place("cols", [P, N_COLS], F32)
        mean_of = place("mean_of", [P, P], F32)
        ident = place("ident", [P, P], F32)
        ident_bf = place("ident_bf", [P, P], BF16)
        mask_bf = place("mask_bf", [P, P], BF16)
        waiter = place("waiter", [P, 1], F32)
        total = place("total", [P, SEQ], F32)
        spread = place("spread", [P, SEQ], F32)
        square = place("square", [P, 2, SEQ], F32)
        tmp = place("tmp", [P, 4, SEQ], F32)
        shared = at[0]
        a = [shared]
        h_hi = place("h_hi", [P, FT, SEQ], F32R, a)
        h_lo = place("h_lo", [P, FT, SEQ], F32R, a)
        a = [shared]
        mix_hi = place("mix_hi", [P, KT, SEQ], F32R, a)
        mix_lo = place("mix_lo", [P, KT, SEQ], F32R, a)
        b = list(a)
        q_ext = place("q_ext", [P, 2, SEQ], F32, a)
        k_ext = place("k_ext", [P, 2, SEQ], F32, a)
        v_chan = place("v_chan", [P, SEQ], F32, a)
        v_tok = place("v_tok", [P, QT, P], F32, a)
        tri = QT * (QT + 1) // 2 * P
        probs = place("probs", [P, 2, tri], F32, a)
        probs_t = place("probs_t", [P, tri], F32, a)
        fg = place("fg", [HEADS, 4, SEQ], F32, a)
        wf = place("wf", [P, KT, HEADS], F32, a)
        bf = place("bf", [HEADS, 1], F32, a)
        stat = place("stat", [P, 2, 12], F32, a)
        a = list(b)
        w_ai = place("w_ai", [P, 2, 2 * P], F32, a)
        conv_x = place("conv_x", [P, SEQ], F32, a)
        gate_r = place("gate_r", [P, SEQ], F32, a)
        gate_i = place("gate_i", [P, SEQ], F32, a)
        half_t = place("half_t", [P, SEQ], F32, a)
        inv_t = place("inv_t", [P, SEQ], F32, a)
        decay = place("decay", [P, SEQ], F32, a)
        drive = place("drive", [P, SEQ], F32, a)
        state = place("state", [P, SEQ], F32, a)
        gelu_g = place("gelu_g", [P, SEQ], F32, a)
        lam4 = place("lam4", [P, 6, KT], F32, a)
        a = [b[0] + 4 * 4 * P]
        p_in = place("p_in", [P, 2, SEQ], F32, a)
        p_hi = place("p_hi", [P, 2, SEQ], F32R, a)
        p_lo = place("p_lo", [P, 2, SEQ], F32R, a)
        emb = place("emb", [P, KT, SEQ], F32, a)

        banks = [ctx.enter_context(nc.psum_tensor(f"bank{n}", [P, SEQ], F32)) for n in range(8)]
        c_dram = nc.dram_tensor("forget_rows", (HEADS, SEQ), F32, kind="Internal").ap()

        unit_loaded = [sem(f"unit_loaded{s}") for s in range(SLOTS)]
        unit_split = sem("unit_split")
        unit_used = sem("unit_used")
        inputs_loaded = sem("inputs_loaded")
        consts_set = sem("consts_set")
        x_hi_ready, x_lo_ready = sem("x_hi_ready"), sem("x_lo_ready")
        mix_hi_ready, mix_lo_ready = sem("mix_hi_ready"), sem("mix_lo_ready")
        fg_done, fg_abs, fg_exp, fg_rows = sem("fg_done"), sem("fg_abs"), sem("fg_exp"), sem("fg_rows")
        fg_stored, row_loaded = sem("fg_stored"), sem("row_loaded")
        q_read, kv_read = sem("q_read"), sem("kv_read")
        vt_done, vt_read = sem("vt_done"), sem("vt_read")
        s_done, max_ready, exp_ready, probs_ready = (sem("s_done"), sem("max_ready"), sem("exp_ready"),
                                                     sem("probs_ready"))
        pt_done, pt_read, pv_done = sem("pt_done"), sem("pt_read"), sem("pv_done")
        o_read = sem("o_read")
        tile_read = {n: sem(f"{n}_read") for n in phases if n not in ("qkv", "rg")}
        sum_ready, mean_done, centred, squared, var_done, dev_ready, scaled, stat_read = (
            sem(n) for n in ("sum_ready", "mean_done", "centred", "squared", "var_done", "dev_ready",
                             "scaled", "stat_read"))
        x_ready, conv_first, conv_done, gelu_done, h_ready, h_hi_ready, h_lo_ready = (
            sem(n) for n in ("x_ready", "conv_first", "conv_done", "gelu_done", "h_ready", "h_hi_ready",
                             "h_lo_ready"))
        p_loaded, p_hi_ready, p_lo_ready, gated, emb_added = (
            sem(n) for n in ("p_loaded", "p_hi_ready", "p_lo_ready", "gated", "emb_added"))
        lru_w_loaded = [sem(f"lru_w_loaded{n}") for n in range(2)]
        lam_exp, lam_abs = sem("lam_exp"), sem("lam_abs")
        rg_first, rg_conv, rg_gates, rg_sig, rg_tanh, rg_sqrt, rg_gelu, rg_y = (
            sem(n) for n in ("rg_first", "rg_conv", "rg_gates", "rg_sig", "rg_tanh", "rg_sqrt", "rg_gelu",
                             "rg_y"))
        rg_x_read, rg_g_read, emb_done = sem("rg_x_read"), sem("rg_g_read"), sem("emb_done")
        stored = sem("stored")

        block = ctx.enter_context(nc.Block())

        def used(ph, i, r):
            return ph.unit(i, r) + (LEAD + 1)

        def tail(widths, r):
            return sum(widths[:r % 3])

        @block.sync
        def _(sp):
            sp.dma_start(x[:], xT).then_inc(inputs_loaded, 16)
            sp.dma_start(cols[:], columns).then_inc(inputs_loaded, 16)
            sp.dma_start(wf[:], w_forget).then_inc(inputs_loaded, 16)
            sp.dma_start(bf[:], b_forget).then_inc(inputs_loaded, 16)
            square_first = [0]
            for name, ph in phases.items():
                base = square_first[0]
                n = len(ph.slots)
                with sp.Fori(0, ph.iters) as i:
                    for r, s in enumerate(ph.slots):
                        sp.wait_ge(unit_split, ph.unit(i, r) + 1)
                        w = ph.widths[r]
                        if name.startswith("down"):
                            c = tail(ph.widths, r)
                            src = w_down[bass.ds(i * (n // 3) + (int(name[-1]) * KT + r // 3), 1), :, c:c + w]
                        else:
                            src = w_square[bass.ds(i * n + (base + r), 1), :, :]
                        sp.dma_start(stage[:, s, 0:w],
                                     src.rearrange("a p n -> (a p) n")).then_inc(unit_loaded[s], 16)
                        if name == "rg" and r % 2:
                            sp.wait_ge(rg_gates, i * 2 + (r // 2 + 1))
                            sp.dma_start(w_ai[:, r // 2, :], w_lru[bass.ds(i * 2 + r // 2, 1), :, :]
                                         .rearrange("a p n -> (a p) n")).then_inc(lru_w_loaded[r // 2], 16)
                if not name.startswith("down"):
                    square_first[0] += ph.iters * n
            for m in range(KT):
                sp.wait_ge(emb_added, 4 + KT + m + 1)
                sp.dma_start(outT[m], x[:, m, :]).then_inc(stored, 16)
            sp.wait_ge(stored, 16 * KT)

        @block.gpsimd
        def _(pool):
            pool.sem_inc(unit_split, LEAD)
            pool.memset(waiter[:], 0.0)
            pool.memset(mean_of[:], 1.0 / D_MODEL)
            pool.memset(ident[:], 1.0)
            pool.memset(ident_bf[:], 1.0)
            pool.memset(mask_bf[:], 0.0)
            pool.drain()
            pool.memset(q_ext[HEAD_DIM:HEAD_DIM + 1, :, :], 1.0)
            pool.drain()
            for m in (ident, ident_bf):
                pool.affine_select(out=m[:], in_=m[:], compare_op=ALU.is_equal, fill=0.0, base=0,
                                   pattern=[[-1, P]], channel_multiplier=1)
            pool.affine_select(out=mask_bf[:], in_=mask_bf[:], compare_op=ALU.is_ge, fill=MASKED, base=0,
                               pattern=[[-1, P]], channel_multiplier=1)
            pool.drain()
            pool.sem_inc(consts_set, 1)
            for ph in phases.values():
                with pool.Fori(0, ph.iters) as i:
                    for r, s in enumerate(ph.slots):
                        w = ph.widths[r]
                        pool.wait_ge(unit_loaded[s], ph.uses(i, r) * 16)
                        pool.wait_ge(unit_used, ph.unit(i, r) + 1)
                        pool.tensor_tensor(waiter[:], waiter[:], waiter[:], ALU.mult)
                        pool.drain()
                        pool.tensor_scalar(w_hi[:, s, 0:w], stage[:, s, 0:w], 1.0, 0.0, ALU.mult, ALU.add)
                        pool.drain()
                        pool.tensor_tensor(w_lo[:, s, 0:w], stage[:, s, 0:w], w_hi[:, s, 0:w].bitcast(F32),
                                           ALU.subtract).then_inc(unit_split, 1)

        @block.tensor
        def _(pe):
            pe.sem_inc(unit_used, LEAD)

            def unit_ready(ph, i, r):
                pe.wait_ge(unit_split, ph.unit(i, r) + (1 + LEAD))

            def three(out, s, c, m_hi, m_lo, first, last):
                pe.matmul(out, w_hi[:, s, c:c + P], m_hi, start=first, stop=False)
                pe.matmul(out, w_hi[:, s, c:c + P], m_lo, start=False, stop=False)
                return pe.matmul(out, w_lo[:, s, c:c + P], m_hi, start=False, stop=last)

            def whole_tile(ph, i, r, bank, hi, lo):
                unit_ready(ph, i, r)
                for k in range(KT):
                    mm = three(banks[bank][:], ph.slots[r], k * P, hi[:, k, :], lo[:, k, :], k == 0, k == KT - 1)
                mm.then_inc(unit_used, 1)

            def norm_sums(n):
                pe.wait_ge(sum_ready, n + 1)
                pe.matmul(banks[6][:], mean_of[:], total[:], start=True, stop=True).then_inc(mean_done, 1)
                for m in range(KT):
                    pe.wait_ge(squared, n * KT + m + 1)
                    mm = pe.matmul(banks[7][:], mean_of[:], square[:, m % 2, :], start=(m == 0),
                                   stop=(m == KT - 1))
                    mm.then_inc(var_done, 1)

            pe.wait_ge(inputs_loaded, 64)
            pe.wait_ge(consts_set, 1)
            for k in range(KT):
                mm = pe.matmul(banks[0][0:HEADS, :], wf[:, k, :], x[:, k, :], start=(k == 0), stop=(k == KT - 1))
            mm.then_inc(fg_done, 1)

            qkv = phases["qkv"]
            S_AT = [(3, 384), (4, 0), (3, 0), (2, 0)]

            def project(j, r, bank):
                whole_tile(qkv, j, r, bank, x_hi, x_lo)

            def scores(j, h):
                pe.wait_ge(exp_ready, j * 8 + (h * 4))
                if h == 0:
                    pe.wait_ge(q_read, j + 1)
                    pe.wait_ge(kv_read, j * 2 + 2)
                    pe.wait_ge(row_loaded, j * 16 + 16)
                for t in (3, 2, 0, 1):
                    bank, c = S_AT[t]
                    w = (t + 1) * P
                    pe.matmul(banks[bank][:, c:c + w], q_ext[0:HEAD_DIM + 1, h, t * P:(t + 1) * P],
                              k_ext[0:HEAD_DIM + 1, h, 0:w], start=True, stop=False, skip_group_check=True)
                    mm = pe.matmul(banks[bank][:, c + w - P:c + w], ident_bf[:], mask_bf[:], start=False,
                                   stop=True, skip_group_check=True)
                mm.then_inc(s_done, 1)

            PT_AT = [(5, 0), (6, 0), (5, 0), (5, 256)]

            def weigh(j, h):
                pe.wait_ge(probs_ready, j * 2 + (h + 1))
                for step, tiles in enumerate(((0,), (1,), (2, 3))):
                    if step == 0:
                        pe.wait_ge(pt_read, j * 6 + (h * 3 + 1))
                    if step == 1:
                        pe.wait_ge(pt_read, j * 6 + (h * 3 + 1))
                    if step == 2:
                        pe.wait_ge(pt_read, j * 6 + (h * 3 + 2))
                    for kt in tiles:
                        bank, c = PT_AT[kt]
                        for t in range(kt, QT):
                            a0 = (t * (t + 1) // 2 + kt) * P
                            mm = pe.transpose(banks[bank][:, c + (t - kt) * P:c + (t - kt + 1) * P],
                                              probs[:, h, a0:a0 + P], ident[:])
                    mm.then_inc(pt_done, 1)
                if h == 0:
                    pe.wait_ge(o_read, j + 1)
                    pe.wait_ge(vt_read, j + 1)
                c0 = 0
                for kt in range(QT):
                    w = (QT - kt) * P
                    pe.wait_ge(pt_read, j * 6 + (h * 3 + min(kt, 2) + 2))
                    mm = pe.matmul(banks[7][h * HEAD_DIM:(h + 1) * HEAD_DIM, kt * P:SEQ],
                                   v_tok[:, kt, h * HEAD_DIM:(h + 1) * HEAD_DIM], probs_t[:, c0:c0 + w],
                                   start=(kt == 0), stop=(kt == QT - 1), skip_group_check=True)
                    c0 += w
                mm.then_inc(pv_done, 1)

            def turn_values(j):
                pe.wait_ge(kv_read, j * 2 + 2)
                pe.wait_ge(o_read, j + 1)
                for t in range(QT):
                    mm = pe.transpose(banks[7][:, t * P:(t + 1) * P], v_chan[:, t * P:(t + 1) * P], ident[:])
                mm.then_inc(vt_done, 1)

            def attention_round(j, project_it, attend_it):
                if attend_it:
                    turn_values(j - 1)
                    scores(j - 1, 0)
                if project_it:
                    project(j, 0, 0)
                if attend_it:
                    scores(j - 1, 1)
                if project_it:
                    project(j, 1, 1)
                if attend_it:
                    weigh(j - 1, 0)
                if project_it:
                    pe.wait_ge(q_read, j + 1)
                    project(j, 2, 0)
                if attend_it:
                    weigh(j - 1, 1)

            pe.wait_ge(x_lo_ready, KT)
            pe.wait_ge(fg_abs, 1)
            attention_round(0, True, False)
            with pe.Fori(1, PAIRS) as j:
                pe.wait_ge(kv_read, j * 2)
                attention_round(j, True, True)
            attention_round(PAIRS, False, True)

            def square_phase(name, hi, lo, ready):
                ph = phases[name]
                for sem_, count in ready:
                    pe.wait_ge(sem_, count)
                n = len(ph.slots)
                with pe.Fori(0, ph.iters) as i:
                    for r in range(n):
                        pe.wait_ge(tile_read[name], i * n + (r + 1))
                        whole_tile(ph, i, r, r, hi, lo)

            def down_phase(name, layer):
                ph = phases[name]
                pe.wait_ge(h_lo_ready, (layer + 1) * FT + 2)
                with pe.Fori(0, ph.iters) as i:
                    for half in range(2):
                        pe.wait_ge(tile_read[name], i * 2 + (half + 1))
                        k = 0
                        for part in range(3):
                            r = half * 3 + part
                            unit_ready(ph, i, r)
                            for c in range(ph.widths[r] // P):
                                mm = three(banks[half][:], ph.slots[r], c * P, h_hi[:, k, :], h_lo[:, k, :],
                                           k == 0, k == FT - 1)
                                k += 1
                            mm.then_inc(unit_used, 1)

            def ple_phase(name, layer):
                ph = phases[name]
                pe.wait_ge(p_lo_ready, (layer + 1) * 2)
                for r in range(2):
                    unit_ready(ph, 0, r)
                    for c in range(4):
                        m = r * 4 + c
                        if m >= 6:
                            pe.wait_ge(tile_read[name], m - 6 + 1)
                        for k in range(2):
                            mm = three(banks[m % 6][:], ph.slots[r], (c * 2 + k) * P, p_hi[:, k, :],
                                       p_lo[:, k, :], k == 0, k == 1)
                        mm.then_inc(emb_done, 1)
                    pe.wait_ge(emb_done, layer * KT + (r + 1) * 4)
                    pe.sem_inc(unit_used, 1)
                pe.wait_ge(tile_read[name], KT)

            def rest_of_layer(layer):
                pe.wait_ge(mix_lo_ready, (layer + 1) * KT)
                square_phase(f"out{layer}", mix_hi, mix_lo, [])
                norm_sums(2 * layer)
                square_phase(f"up{layer}", x_hi, x_lo, [(x_lo_ready, (layer * 3 + 2) * KT)])
                down_phase(f"down{layer}", layer)
                norm_sums(2 * layer + 1)
                ple_phase(f"ple{layer}", layer)
                square_phase(f"gate{layer}", x_hi, x_lo, [(x_lo_ready, (layer * 3 + 3) * KT)])

            rest_of_layer(0)

            rg = phases["rg"]
            pe.wait_ge(x_lo_ready, 4 * KT)
            pe.wait_ge(tile_read["gate0"], 4 + KT)
            pe.sem_inc(rg_gates, 2)
            with pe.Fori(0, rg.iters) as i:
                for half in range(2):
                    for part in range(2):
                        r = half * 2 + part
                        pe.wait_ge((rg_x_read, rg_g_read)[part], i * 2 + (half + 1))
                        whole_tile(rg, i, r, r, x_hi, x_lo)
                    pe.wait_ge(rg_conv, i * 2 + (half + 1))
                    pe.wait_ge(lru_w_loaded[half], (i + 1) * 16)
                    pe.wait_ge(rg_sig, i * 2 + (half + 1))
                    pe.matmul(banks[4][:], w_ai[:, half, 0:P], conv_x[:], start=True, stop=True)
                    pe.matmul(banks[5][:], w_ai[:, half, P:2 * P], conv_x[:], start=True,
                              stop=True).then_inc(rg_gates, 1)
            rest_of_layer(1)

        @block.vector
        def _(dve):
            def log1p_twice(q, e, den, q2, acc):
                dve.tensor_scalar(den, e, 2.0, None, ALU.add)
                dve.drain()
                dve.reciprocal(q2, den)
                dve.drain()
                dve.tensor_tensor(q, e, q2, ALU.mult)
                dve.drain()
                dve.tensor_tensor(q2, q, q, ALU.mult)
                dve.drain()
                dve.tensor_scalar(acc, q2, LOG1P_TERMS[-1], None, ALU.mult)
                dve.drain()
                for c in LOG1P_TERMS[-2:0:-1]:
                    dve.scalar_tensor_tensor(acc, acc, c, q2, ALU.add, ALU.mult)
                    dve.drain()
                dve.scalar_tensor_tensor(acc, acc, LOG1P_TERMS[0], q, ALU.add, ALU.mult)
                dve.drain()

            def layer_norm(n, layer, g):
                dve.drain()
                dve.sem_inc(sum_ready, 1)
                dve.wait_ge(mean_done, n + 1)
                for m in range(KT):
                    dve.tensor_tensor(x[:, m, :], x[:, m, :], banks[6][:], ALU.subtract).then_inc(centred, 1)
                dve.wait_ge(dev_ready, n + 1)
                dve.drain()
                dve.reciprocal(spread[:], spread[:])
                dve.drain()
                for m in range(KT + 1):
                    if m < KT:
                        c = COLS[g, layer] + m
                        dve.scalar_tensor_tensor(x[:, m, :], x[:, m, :], cols[:, c:c + 1], spread[:], ALU.mult,
                                                 ALU.mult).then_inc(scaled, 1)
                    if m > 0:
                        dve.wait_ge(x_hi_ready, (x_round[0] * KT) + m)
                        dve.tensor_tensor(x_lo[:, m - 1, :], x[:, m - 1, :], x_hi[:, m - 1, :].bitcast(F32),
                                          ALU.subtract).then_inc(x_lo_ready, 1)
                x_round[0] += 1

            x_round = [0]

            def residual_phase(name, per_round, units):
                dve.drain()
                dve.memset(total[:], 0.0)
                with dve.Fori(0, KT // per_round) as i:
                    for r in range(per_round):
                        dve.wait_ge(unit_used, used(phases[name], i, (r + 1) * units - 1))
                        xm = x[:, bass.ds(i * per_round + r, 1), :].rearrange("p a n -> p (a n)")
                        dve.scalar_tensor_tensor(xm, xm, ALPHA, banks[r][:], ALU.mult,
                                                 ALU.add).then_inc(tile_read[name], 1)
                        dve.drain()
                        dve.tensor_tensor(total[:], total[:], xm, ALU.add)

            dve.wait_ge(inputs_loaded, 64)
            for m in range(KT):
                dve.wait_ge(x_hi_ready, m + 1)
                dve.tensor_tensor(x_lo[:, m, :], x[:, m, :], x_hi[:, m, :].bitcast(F32),
                                  ALU.subtract).then_inc(x_lo_ready, 1)
            x_round[0] = 1

            dve.wait_ge(fg_done, 1)
            z, e, r0, r1 = (fg[:, n, :] for n in range(4))
            dve.tensor_scalar(z, banks[0][0:HEADS, :], bf[:, 0:1], None, ALU.add)
            dve.drain()
            dve.scalar_tensor_tensor(e, z, -1.0, z, ALU.mult, ALU.max).then_inc(fg_abs, 1)
            dve.wait_ge(fg_exp, 1)
            log1p_twice(r0, e, r1, r1, total[0:HEADS, :])
            dve.tensor_scalar(z, z, -1.0, 0.0, ALU.mult, ALU.max)
            dve.memset(r0, 1.0)
            dve.drain()
            dve.scalar_tensor_tensor(e, total[0:HEADS, :], 2.0, z, ALU.mult, ALU.add)
            dve.drain()
            dve.tensor_tensor_scan(r1, r0, e, 0.0, ALU.mult, ALU.add).then_inc(fg_rows, 1)

            def queries(j):
                dve.wait_ge(unit_used, used(phases["qkv"], j, 0))
                dve.wait_ge(s_done, j * 2)
                for h in range(2):
                    dve.tensor_scalar(q_ext[0:HEAD_DIM, h, :], banks[0][h * HEAD_DIM:(h + 1) * HEAD_DIM, :],
                                      HEAD_DIM ** -0.5, None, ALU.mult)
                dve.drain()
                dve.sem_inc(q_read, 1)

            def maxima(j, h):
                dve.wait_ge(s_done, j * 2 + (h + 1))
                for t, (bank, c) in ((3, (2, 0)), (2, (3, 0)), (0, (3, 384)), (1, (4, 0))):
                    mx = dve.tensor_reduce(stat[:, h, t:t + 1], banks[bank][:, c:c + (t + 1) * P], AX_X, ALU.max,
                                           negate=True)
                    mx.then_inc(max_ready, 1)

            def normalise(j, h):
                dve.wait_ge(exp_ready, j * 8 + (h * 4 + 4))
                dve.reciprocal(stat[:, h, 8:12], stat[:, h, 4:8])
                dve.drain()
                for t in range(QT):
                    a0, w = t * (t + 1) // 2 * P, (t + 1) * P
                    nm = dve.tensor_scalar(probs[:, h, a0:a0 + w], probs[:, h, a0:a0 + w],
                                           stat[:, h, 8 + t:9 + t], None, ALU.mult)
                dve.drain()
                dve.sem_inc(probs_ready, 1)

            def mixed(j):
                dve.wait_ge(mix_hi_ready, j + 1)
                lo = mix_lo[:, bass.ds(j, 1), :].rearrange("p a n -> p (a n)")
                hi = mix_hi[:, bass.ds(j, 1), :].rearrange("p a n -> p (a n)")
                dve.tensor_tensor(lo, banks[7][:], hi.bitcast(F32), ALU.subtract)
                dve.drain()
                dve.sem_inc(mix_lo_ready, 1)
                dve.sem_inc(o_read, 1)

            dve.sem_inc(o_read, 1)
            dve.wait_ge(unit_used, used(phases["qkv"], 0, 0))
            for h in range(2):
                dve.tensor_scalar(q_ext[0:HEAD_DIM, h, :], banks[0][h * HEAD_DIM:(h + 1) * HEAD_DIM, :],
                                  HEAD_DIM ** -0.5, None, ALU.mult)
            dve.drain()
            dve.sem_inc(q_read, 1)
            with dve.Fori(1, PAIRS) as j:
                maxima(j - 1, 0)
                normalise(j - 1, 0)
                maxima(j - 1, 1)
                queries(j)
                normalise(j - 1, 1)
                dve.wait_ge(pv_done, j * 2)
                mixed(j - 1)
            maxima(PAIRS - 1, 0)
            normalise(PAIRS - 1, 0)
            maxima(PAIRS - 1, 1)
            normalise(PAIRS - 1, 1)
            mixed(PAIRS - 1)

            def conv_ffn(layer):
                name = f"up{layer}"
                base = COLS["conv", layer]
                with dve.Fori(0, FT // 2) as i:
                    for half in range(2):
                        for part in (1, 0):
                            r = half * 2 + part
                            c = (i * 4 + r) * (CONV_F + 1) + base
                            t = tmp[:, r, :]
                            dve.wait_ge(conv_first, layer * 2 * FT + i * 4 + (half * 2 + (2 - part)))
                            dve.scalar_tensor_tensor(t[:, 1:SEQ], banks[r][:, 0:SEQ - 1], cols[:, bass.ds(c + 1, 1)],
                                                     t[:, 1:SEQ], ALU.mult, ALU.add)
                            dve.drain()
                            dve.scalar_tensor_tensor(t[:, 2:SEQ], banks[r][:, 0:SEQ - 2], cols[:, bass.ds(c, 1)],
                                                     t[:, 2:SEQ], ALU.mult, ALU.add).then_inc(conv_done, 1)
                            dve.wait_ge(conv_done, layer * 2 * FT + i * 4 + (half * 2 + (2 - part)))
                        dve.sem_inc(tile_read[name], 2)
                        n = layer * FT + i * 2 + (half + 1)
                        dve.wait_ge(gelu_done, n)
                        dve.tensor_tensor(tmp[:, half * 2, :], tmp[:, half * 2, :], tmp[:, half * 2 + 1, :],
                                          ALU.mult).then_inc(h_ready, 1)
                        dve.wait_ge(h_hi_ready, n)
                        lo = h_lo[:, bass.ds(i * 2 + half, 1), :].rearrange("p a n -> p (a n)")
                        hi = h_hi[:, bass.ds(i * 2 + half, 1), :].rearrange("p a n -> p (a n)")
                        dve.tensor_tensor(lo, tmp[:, half * 2, :], hi.bitcast(F32), ALU.subtract)\
                            .then_inc(h_lo_ready, 1)

            def embed(layer):
                for k in range(2):
                    dve.wait_ge(p_hi_ready, layer * 2 + k + 1)
                    dve.tensor_tensor(p_lo[:, k, :], p_in[:, k, :], p_hi[:, k, :].bitcast(F32),
                                      ALU.subtract).then_inc(p_lo_ready, 1)

            def gate(layer):
                last = layer == DEPTH - 1
                with dve.Fori(0, 2) as i:
                    for r in range(4):
                        m = i * 4 + r
                        xm = x[:, bass.ds(m, 1), :].rearrange("p a n -> p (a n)")
                        dve.wait_ge(gated, i * 4 + (layer * KT + r + 1))
                        dve.tensor_tensor(tmp[:, r, :], tmp[:, r, :],
                                          emb[:, bass.ds(m, 1), :].rearrange("p a n -> p (a n)"), ALU.mult)
                        dve.drain()
                        dve.tensor_tensor(xm, xm, tmp[:, r, :], ALU.add).then_inc(emb_added, 1)
                dve.drain()
                if not last:
                    for m in range(KT):
                        dve.wait_ge(x_hi_ready, x_round[0] * KT + m + 1)
                        dve.tensor_tensor(x_lo[:, m, :], x[:, m, :], x_hi[:, m, :].bitcast(F32),
                                          ALU.subtract).then_inc(x_lo_ready, 1)
                    x_round[0] += 1

            def rest_of_layer(layer):
                dve.sem_inc(tile_read[f"out{layer}"], 4)
                residual_phase(f"out{layer}", 4, 1)
                dve.sem_inc(tile_read[f"up{layer}"], 4)
                layer_norm(2 * layer, layer, "ln1_g")
                conv_ffn(layer)
                dve.sem_inc(tile_read[f"down{layer}"], 2)
                residual_phase(f"down{layer}", 2, 3)
                layer_norm(2 * layer + 1, layer, "ln2_g")
                embed(layer)
                gate(layer)

            dve.sem_inc(h_lo_ready, 2)
            dve.sem_inc(emb_added, 4)
            rest_of_layer(0)

            lz, le, l0, l1, l2 = (lam4[:, n, :] for n in range(5))
            c = COLS["rg_lam"]
            dve.drain()
            dve.tensor_scalar(lz, cols[:, c:c + KT], -1.0, None, ALU.mult)
            dve.drain()
            dve.tensor_tensor(le, lz, cols[:, c:c + KT], ALU.max).then_inc(lam_abs, 1)
            dve.wait_ge(lam_exp, 1)
            log1p_twice(l0, le, l1, l1, l2)
            dve.tensor_scalar(lz, lz, 0.0, 4.0, ALU.max, ALU.mult)
            dve.drain()
            dve.scalar_tensor_tensor(lam4[:, 5, :], l2, 8.0, lz, ALU.mult, ALU.add)
            dve.drain()
            dve.sem_inc(lam_abs, 1)
            dve.sem_inc(rg_x_read, 2)
            dve.sem_inc(rg_y, 1)
            with dve.Fori(0, KT // 2) as i:
                for half in range(2):
                    n = i * 2 + (half + 1)
                    c = (i * 2 + half) * (CONV_B + 1) + COLS["rg_conv"]
                    dve.wait_ge(rg_first, n)
                    for lag in range(1, CONV_B):
                        dve.scalar_tensor_tensor(conv_x[:, lag:SEQ], banks[half * 2][:, 0:SEQ - lag],
                                                 cols[:, bass.ds(c + (CONV_B - 1 - lag), 1)], conv_x[:, lag:SEQ],
                                                 ALU.mult, ALU.add)
                        dve.drain()
                    dve.sem_inc(rg_x_read, 1)
                    dve.sem_inc(rg_conv, 1)
                    dve.wait_ge(rg_tanh, n)
                    dve.tensor_scalar(inv_t[:], half_t[:], 1.0, None, ALU.add)
                    dve.tensor_scalar(decay[:], half_t[:], -1.0, 1.0, ALU.mult, ALU.add)
                    dve.drain()
                    dve.reciprocal(inv_t[:], inv_t[:])
                    dve.tensor_tensor(gate_i[:], gate_i[:], conv_x[:], ALU.mult)
                    dve.drain()
                    dve.tensor_tensor(decay[:], decay[:], inv_t[:], ALU.mult)
                    dve.wait_ge(rg_sqrt, n)
                    dve.scalar_tensor_tensor(drive[:], gate_r[:], 2.0, inv_t[:], ALU.mult, ALU.mult)
                    dve.drain()
                    dve.tensor_tensor(drive[:], drive[:], gate_i[:], ALU.mult)
                    dve.drain()
                    dve.tensor_tensor_scan(state[:], decay[:], drive[:], 0.0, ALU.mult, ALU.add)
                    dve.drain()
                    dve.wait_ge(rg_gelu, n)
                    dve.tensor_tensor(state[:], state[:], gelu_g[:], ALU.mult).then_inc(rg_y, 1)
                    dve.wait_ge(mix_hi_ready, n + KT)
                    lo = mix_lo[:, bass.ds(i * 2 + half, 1), :].rearrange("p a n -> p (a n)")
                    hi = mix_hi[:, bass.ds(i * 2 + half, 1), :].rearrange("p a n -> p (a n)")
                    dve.tensor_tensor(lo, state[:], hi.bitcast(F32), ALU.subtract)
                    dve.drain()
                    dve.sem_inc(mix_lo_ready, 1)
            rest_of_layer(1)

        @block.scalar
        def _(act):
            x_round = [0]

            def layer_norm(n, layer, b):
                for m in range(KT):
                    act.wait_ge(centred, n * KT + m + 1)
                    if m >= 2:
                        act.wait_ge(var_done, n * KT + m - 1)
                    act.activation(square[:, m % 2, :], x[:, m, :], ACT.Square).then_inc(squared, 1)
                act.wait_ge(var_done, (n + 1) * KT)
                act.activation(spread[:], banks[7][:], ACT.Sqrt, bias=LN_EPS).then_inc(dev_ready, 1)
                for m in range(KT):
                    c = COLS[b, layer] + m
                    act.wait_ge(scaled, n * KT + m + 1)
                    act.activation(x[:, m, :], x[:, m, :], ACT.Identity, bias=cols[:, c:c + 1])
                    act.drain()
                    act.copy(x_hi[:, m, :], x[:, m, :]).then_inc(x_hi_ready, 1)
                x_round[0] += 1

            act.wait_ge(inputs_loaded, 64)
            for m in range(KT):
                act.copy(x_hi[:, m, :], x[:, m, :]).then_inc(x_hi_ready, 1)
            x_round[0] = 1

            act.wait_ge(fg_abs, 1)
            act.activation(fg[:, 1, :], fg[:, 1, :], ACT.Exp, scale=-1.0).then_inc(fg_exp, 1)
            act.wait_ge(fg_rows, 1)
            act.dma_start(c_dram, fg[:, 3, :]).then_inc(fg_stored, 16)
            act.wait_ge(fg_stored, 16)

            def keys(j, scored):
                act.wait_ge(unit_used, used(phases["qkv"], j, 1))
                if scored:
                    act.wait_ge(s_done, j * 2)
                act.dma_start(k_ext[HEAD_DIM:HEAD_DIM + 1, :, :],
                              c_dram.rearrange("(j h) n -> j h n", h=2)[bass.ds(j, 1), :, :]).then_inc(row_loaded, 16)
                for h in range(2):
                    act.copy(k_ext[0:HEAD_DIM, h, :], banks[1][h * HEAD_DIM:(h + 1) * HEAD_DIM, :])
                act.drain()
                act.sem_inc(kv_read, 1)

            def values(j, turned):
                act.wait_ge(unit_used, used(phases["qkv"], j, 2))
                if turned:
                    act.wait_ge(vt_done, j)
                act.copy(v_chan[:], banks[0][:]).then_inc(kv_read, 1)

            def token_values(j):
                act.wait_ge(vt_done, j + 1)
                act.copy(v_tok[:].rearrange("p t c -> p (t c)"), banks[7][:]).then_inc(vt_read, 1)

            def exponentials(j, h, weighed):
                if weighed:
                    act.wait_ge(pt_done, j * 6 - (3 - h * 3))
                for n, (t, (bank, c)) in enumerate(((3, (2, 0)), (2, (3, 0)), (0, (3, 384)), (1, (4, 0)))):
                    act.wait_ge(max_ready, j * 8 + (h * 4 + max(n + 1, 3 if n in (1, 2) else 0)))
                    a0, w = t * (t + 1) // 2 * P, (t + 1) * P
                    act.activation(probs[:, h, a0:a0 + w], banks[bank][:, c:c + w], ACT.Exp,
                                   bias=stat[:, h, t:t + 1], accum_out=stat[:, h, 4 + t:5 + t])
                    act.drain()
                    act.sem_inc(exp_ready, 1)

            def turned_probs(j, h, weighed):
                for step, (bank, a0, w) in enumerate(((5, 0, 512), (6, 512, 384), (5, 896, 384))):
                    act.wait_ge(pt_done, j * 6 + (h * 3 + step + 1))
                    if step == 0 and weighed:
                        act.wait_ge(pv_done, j * 2 + h)
                    act.copy(probs_t[:, a0:a0 + w], banks[bank][:, 0:w]).then_inc(pt_read, 1)

            def outputs(j):
                act.wait_ge(pv_done, j * 2 + 2)
                act.copy(mix_hi[:, bass.ds(j, 1), :].rearrange("p a n -> p (a n)"), banks[7][:])\
                    .then_inc(mix_hi_ready, 1)

            def attend(j, j_next, project_it, first):
                token_values(j)
                exponentials(j, 0, not first)
                exponentials(j, 1, not first)
                if project_it:
                    keys(j_next, True)
                turned_probs(j, 0, not first)
                if project_it:
                    values(j_next, True)
                turned_probs(j, 1, True)
                outputs(j)

            act.sem_inc(pt_read, 1)
            keys(0, False)
            values(0, False)
            attend(0, 1, True, True)
            with act.Fori(2, PAIRS) as j:
                attend(j - 1, j, True, False)
            attend(PAIRS - 1, None, False, False)

            def conv_ffn(layer):
                name = f"up{layer}"
                base = COLS["conv", layer]
                with act.Fori(0, FT // 2) as i:
                    for half in range(2):
                        act.wait_ge(unit_used, used(phases[name], i, half * 2 + 1))
                        act.wait_ge(h_lo_ready, i * 2 + (layer * FT + half + 1))
                        for part in (1, 0):
                            r = half * 2 + part
                            c = (i * 4 + r) * (CONV_F + 1) + base
                            act.activation(tmp[:, r, :], banks[r][:], ACT.Identity, bias=cols[:, bass.ds(c + 3, 1)],
                                           scale=cols[:, bass.ds(c + 2, 1)]).then_inc(conv_first, 1)
                        act.wait_ge(conv_done, i * 4 + (layer * 2 * FT + half * 2 + 1))
                        act.activation(tmp[:, half * 2 + 1, :], tmp[:, half * 2 + 1, :],
                                       ACT.Gelu_apprx_tanh).then_inc(gelu_done, 1)
                        act.wait_ge(h_ready, i * 2 + (layer * FT + half + 1))
                        act.copy(h_hi[:, bass.ds(i * 2 + half, 1), :].rearrange("p a n -> p (a n)"),
                                 tmp[:, half * 2, :]).then_inc(h_hi_ready, 1)

            def embed(layer):
                act.dma_start(p_in[:], pT[layer]).then_inc(p_loaded, 16)
                act.wait_ge(p_loaded, 16 * (layer + 1))
                for k in range(2):
                    act.copy(p_hi[:, k, :], p_in[:, k, :]).then_inc(p_hi_ready, 1)
                for m in range(KT):
                    act.wait_ge(emb_done, layer * KT + m + 1)
                    act.copy(emb[:, m, :], banks[m % 6][:]).then_inc(tile_read[f"ple{layer}"], 1)

            def gate(layer):
                name = f"gate{layer}"
                act.sem_inc(tile_read[name], 4)
                with act.Fori(0, 2) as i:
                    for r in range(4):
                        act.wait_ge(unit_used, used(phases[name], i, r))
                        act.wait_ge(emb_added, i * 4 + (layer * KT + r + 1))
                        act.activation(tmp[:, r, :], banks[r][:], ACT.Sigmoid,
                                       bias=cols[:, bass.ds(i * 4 + (COLS["gate_b", layer] + r), 1)])\
                            .then_inc(gated, 1)
                        act.drain()
                        act.sem_inc(tile_read[name], 1)
                if layer < DEPTH - 1:
                    for m in range(KT):
                        act.wait_ge(emb_added, 4 + layer * KT + m + 1)
                        act.copy(x_hi[:, m, :], x[:, m, :]).then_inc(x_hi_ready, 1)

            def rest_of_layer(layer):
                layer_norm(2 * layer, layer, "ln1_b")
                conv_ffn(layer)
                layer_norm(2 * layer + 1, layer, "ln2_b")
                embed(layer)
                gate(layer)

            rest_of_layer(0)

            act.wait_ge(lam_abs, 1)
            act.activation(lam4[:, 1, :], lam4[:, 1, :], ACT.Exp, scale=-1.0).then_inc(lam_exp, 1)
            act.wait_ge(lam_abs, 2)
            act.sem_inc(rg_sig, 1)
            act.sem_inc(rg_g_read, 2)
            rg = phases["rg"]
            with act.Fori(0, rg.iters) as i:
                for half in range(2):
                    m = i * 2 + half
                    n = i * 2 + (half + 1)
                    c = m * (CONV_B + 1) + COLS["rg_conv"]
                    act.wait_ge(unit_used, used(rg, i, half * 2))
                    act.wait_ge(rg_y, n)
                    act.activation(conv_x[:], banks[half * 2][:], ACT.Identity,
                                   bias=cols[:, bass.ds(c + CONV_B, 1)],
                                   scale=cols[:, bass.ds(c + (CONV_B - 1), 1)]).then_inc(rg_first, 1)
                    act.wait_ge(rg_gates, i * 2 + (half + 3))
                    act.activation(gate_r[:], banks[4][:], ACT.Sigmoid, bias=cols[:, bass.ds(m + COLS["rg_ba"], 1)])
                    act.activation(gate_i[:], banks[5][:], ACT.Sigmoid, bias=cols[:, bass.ds(m + COLS["rg_bi"], 1)])
                    act.drain()
                    act.sem_inc(rg_sig, 1)
                    act.activation(half_t[:], gate_r[:], ACT.Tanh,
                                   scale=lam4[:, 5, bass.ds(m, 1)]).then_inc(rg_tanh, 1)
                    act.drain()
                    act.activation(gate_r[:], half_t[:], ACT.Sqrt).then_inc(rg_sqrt, 1)
                    act.wait_ge(unit_used, used(rg, i, half * 2 + 1))
                    act.activation(gelu_g[:], banks[half * 2 + 1][:], ACT.Gelu_apprx_tanh).then_inc(rg_gelu, 1)
                    act.drain()
                    act.sem_inc(rg_g_read, 1)
                    act.wait_ge(rg_y, i * 2 + (half + 2))
                    act.copy(mix_hi[:, bass.ds(m, 1), :].rearrange("p a n -> p (a n)"), state[:])\
                        .then_inc(mix_hi_ready, 1)
            rest_of_layer(1)


def _tiles(w):
    k, n = w.shape[0] // P, w.shape[1] // P
    return w.reshape(k, P, n, P).transpose(2, 1, 0, 3).reshape(n, P, k * P)


def _per_channel(v):
    return v.reshape(-1, P).T


def kernel(**inputs):
    import numpy as np
    import concourse.bacc as bacc
    from concourse.bass_utils import run_bass_kernel_spmd

    g = {k: np.asarray(v) for k, v in inputs.items()}
    w_in = g["a_w_in"][0]
    q, k, v = (_tiles(w_in[:, n * D_MODEL:(n + 1) * D_MODEL]) for n in range(3))
    square = [t for j in range(PAIRS) for t in (q[j], k[j], v[j])] + list(_tiles(g["a_w_out"][0]))

    def rest(layer):
        up = _tiles(g["f_w_up"][layer])
        out = [up[half * FT + j] for j in range(FT) for half in range(2)]
        ple = _tiles(g["ple_w"][layer])
        out += [np.concatenate([ple[4 * n + c] for c in range(4)], axis=1) for n in range(2)]
        return out + list(_tiles(g["ple_gate_w"][layer]))

    square += rest(0)
    rg = _tiles(g["b_w_in"][0])
    square += [rg[half * KT + j] for j in range(KT) for half in range(2)]
    square += list(_tiles(g["b_w_out"][0])) + rest(1)
    columns = []
    for layer in range(DEPTH):
        for name in ("ln1_g", "ln1_b", "ln2_g", "ln2_b", "ple_gate_b"):
            columns.append(_per_channel(g[name][layer]))
        taps = np.stack([*g["f_conv_w"][layer], g["f_conv_b"][layer]])
        taps = taps.reshape(CONV_F + 1, 2, FT, P).transpose(3, 2, 1, 0)
        columns.append(taps.reshape(P, -1))
    taps = np.stack([*g["b_conv_w"][0], g["b_conv_b"][0]]).reshape(CONV_B + 1, KT, P)
    columns.append(taps.transpose(2, 1, 0).reshape(P, -1))
    columns += [_per_channel(g[n][0].reshape(-1)) for n in ("b_b_a", "b_b_i", "b_lam")]

    arrays = {
        "xT": g["x"][0].T.reshape(KT, P, SEQ).transpose(1, 0, 2),
        "pT": g["p"][:, 0].transpose(0, 2, 1).reshape(DEPTH, 2, P, SEQ).transpose(0, 2, 1, 3),
        "w_square": np.stack(square),
        "w_down": np.concatenate([_tiles(g["f_w_down"][layer]) for layer in range(DEPTH)]),
        "w_forget": w_in[:, 3 * D_MODEL:].reshape(KT, P, HEADS).transpose(1, 0, 2),
        "b_forget": g["a_b_f"].reshape(HEADS, 1),
        "w_lru": np.concatenate([g["b_w_a"][0], g["b_w_i"][0]], axis=2),
        "columns": np.concatenate(columns, axis=1),
    }
    arrays = {n: np.ascontiguousarray(a) for n, a in arrays.items()}
    assert arrays["columns"].shape == (P, N_COLS)
    nc = bacc.Bacc("TRN2", target_bir_lowering=False, num_devices=1)
    ins = [nc.dram_tensor(n, a.shape, F32, kind="ExternalInput").ap() for n, a in arrays.items()]
    out = nc.dram_tensor("outT", (KT, P, SEQ), F32, kind="ExternalOutput").ap()
    hybrid_trunk_kernel(nc, *ins, out)
    r = run_bass_kernel_spmd(nc, [arrays], core_ids=[0])
    return np.ascontiguousarray(np.asarray(r.results[0]["outT"]).reshape(D_MODEL, SEQ).T)[None]
```

```python
from contextlib import ExitStack

import concourse.bass as bass
from concourse import mybir

F32 = mybir.dt.float32
F32R = mybir.dt.float32r
BF16 = mybir.dt.bfloat16
ALU = mybir.AluOpType
ACT = mybir.ActivationFunctionType
AX_X = mybir.AxisListType.X

P = 128
SEQ = 512
D_MODEL = 1024
DEPTH = 2
HEADS = 16
HEAD_DIM = D_MODEL // HEADS
D_FF = 2816
D_PLE = 256
CONV_F = 3
CONV_B = 4
LN_EPS = 1e-5
ALPHA = (2.0 * DEPTH) ** 0.25
KT = D_MODEL // P
FT = D_FF // P
PAIRS = HEADS // 2
QT = SEQ // P
UNIT = KT * P
TOGETHER = 5
OUT_TOGETHER = (5, 7)
SHIFT_TILES = 3
SLOTS = 4
TURN_AT = 2
FIRST_AT = (1, 1, 4, 5, 6)
SECOND_AT = (0, 0, 2, 3, 4)
PARTS_AT = 4
PLE_AT = (1, 3)
EMB_READ = (0, 3, 5, 6, 7, 8, 8, 8, 8, 8)
MASKED = -3.0e38
LOG1P_TERMS = [1.0 / (2 * n + 1) for n in range(9)]

COLS = {}


def _columns():
    at = 0
    for layer in range(DEPTH):
        for name, n in (("ln1_g", KT), ("ln1_b", KT), ("ln2_g", KT), ("ln2_b", KT), ("gate_b", KT),
                        ("conv", 2 * FT * (CONV_F + 1))):
            COLS[name, layer] = at
            at += n
    for name, n in (("rg_conv", KT * (CONV_B + 1)), ("rg_ba", KT), ("rg_bi", KT), ("rg_lam", KT)):
        COLS[name] = at
        at += n
    return at


N_COLS = _columns()


class Phase:

    def __init__(self, slots, iters, widths, first, filled, lead):
        self.slots, self.iters, self.widths, self.first, self.filled, self.lead = (
            slots, iters, widths, first, filled, lead)

    def unit(self, i, r):
        return i * len(self.slots) + (self.first + r)

    def fills(self, i, r):
        s = self.slots[r]
        return i * self.slots.count(s) + (self.filled[s] + self.slots[:r + 1].count(s))

    def slot_free(self, i, r):
        return i * len(self.slots) + (self.first + r + 1 + SLOTS - self.lead[r])

    def done(self, i, r):
        return i * len(self.slots) + (self.first + r + 1 + SLOTS)


def plan():
    whole = [UNIT]
    down = [8 * P, 7 * P, 7 * P]
    want = [("qkv", [0, 1, 2], PAIRS, whole), ("out0", [0, 1, 2, 3], 2, whole),
            ("up0", [0, 1, 2, 3], 2 * FT // 4, whole), ("down0", [0, 1, 2] * 2, KT // 2, down),
            ("ple0", [0, 1], 1, whole), ("gate0", [2, 3, 0, 1], 2, whole),
            ("rg", [2, 3, 0, 1], 2 * KT // 4, whole), ("out1", [2, 3, 0, 1], 2, whole),
            ("up1", [2, 3, 0, 1], 2 * FT // 4, whole), ("down1", [2, 3, 0] * 2, KT // 2, down),
            ("ple1", [2, 3], 1, whole), ("gate1", [0, 1, 2, 3], 2, whole)]
    phases, first, last, filled = {}, 0, [-SLOTS] * SLOTS, [0] * SLOTS
    for name, slots, iters, widths in want:
        lead = [SLOTS] * len(slots)
        before, at = list(filled), first
        for _ in range(iters):
            for r, s in enumerate(slots):
                lead[r] = min(lead[r], at - last[s])
                last[s] = at
                filled[s] += 1
                at += 1
        phases[name] = Phase(slots, iters, (widths * len(slots))[:len(slots)], first, before, lead)
        first = at
    return phases


def hybrid_trunk_kernel(nc, xT, pT, w_square, w_down, w_forget, b_forget, w_lru, columns, outT):
    phases = plan()
    with ExitStack() as ctx:
        def sem(name):
            return ctx.enter_context(nc.semaphore(name))

        start = (nc.sbuf_base + 63) // 64 * 64
        size = 207 * 1024
        ctx.enter_context(nc.sbuf_tensor("arena", [P, size // 4], F32))
        at = [start]

        def place(name, shape, dt, where=None):
            n = 4 if dt != BF16 else 2
            for k in shape[1:]:
                n *= k
            n = (n + 63) // 64 * 64
            where = at if where is None else where
            t = nc.alloc_sbuf_tensor_at(name, shape, dt, offset=where[0])
            where[0] += n
            assert where[0] <= start + size, name
            return t

        x = place("x", [P, KT, SEQ], F32)
        x_hi_at = at[0]
        x_hi = place("x_hi", [P, KT, SEQ], F32R)
        x_lo = place("x_lo", [P, KT, SEQ], F32R)
        stage = place("stage", [P, SLOTS, UNIT], F32)
        w_hi = place("w_hi", [P, SLOTS, UNIT], F32R)
        w_lo = place("w_lo", [P, SLOTS, UNIT], F32R)
        cols = place("cols", [P, N_COLS], F32)
        mean_of = place("mean_of", [P, P], F32)
        ident = place("ident", [P, P], F32)
        ident_bf = place("ident_bf", [P, P], BF16)
        mask_bf = place("mask_bf", [P, P], BF16)
        waiter = place("waiter", [P, 1], F32)
        lam4 = place("lam4", [P, 6, KT], F32)
        less_shift = place("less_shift", [P, 1], F32)
        norm_stat = place("norm_stat", [P, 2 * QT], F32)
        shift_of = place("shift_of", [P, P], F32)
        part_total = place("part_total", [P, SEQ], F32)
        squares = part_total
        shift = place("shift", [P, SEQ], F32)
        dist = place("dist", [P, 2, SEQ], F32)
        total = place("total", [P, SEQ], F32)
        tmp_at = at[0]
        tmp = place("tmp", [P, 4, SEQ], F32)
        p_in = place("p_in", [P, 2, SEQ], F32, [x_hi_at])
        a = [tmp_at]
        p_hi = place("p_hi", [P, 2, SEQ], F32R, a)
        p_lo = place("p_lo", [P, 2, SEQ], F32R, a)
        shared = at[0]
        a = [shared]
        h_hi = place("h_hi", [P, FT, SEQ], F32R, a)
        h_lo = place("h_lo", [P, FT, SEQ], F32R, a)
        a = [shared]
        mix_hi = place("mix_hi", [P, KT, SEQ], F32R, a)
        mix_lo = place("mix_lo", [P, KT, SEQ], F32R, a)
        b = list(a)
        q_ext = place("q_ext", [P, 2, SEQ], F32, a)
        k_ext = place("k_ext", [P, 2, SEQ], F32, a)
        v_chan = place("v_chan", [P, SEQ], F32, a)
        v_tok = place("v_tok", [P, QT, P], F32, a)
        tri = QT * (QT + 1) // 2 * P
        probs = place("probs", [P, 2, tri], F32, a)
        probs_t = place("probs_t", [P, tri], F32, a)
        fg = place("fg", [HEADS, 4, SEQ], F32, a)
        wf = place("wf", [P, KT, HEADS], F32, a)
        bf = place("bf", [HEADS, 1], F32, a)
        stat = place("stat", [P, 2, 12], F32, a)
        a = list(b)
        w_ai = place("w_ai", [P, 2, 2 * P], F32, a)
        conv_x = place("conv_x", [P, 2, SEQ], F32, a)
        half_t = place("half_t", [P, 2, SEQ], F32, a)
        decay = place("decay", [P, 2, SEQ], F32, a)
        drive = place("drive", [P, SEQ], F32, a)
        state = place("state", [P, 2, SEQ], F32, a)
        gelu_g = place("gelu_g", [P, 2, SEQ], F32, a)
        g = [tmp_at]
        gate_r = place("gate_r", [P, 2, SEQ], F32, g)
        gate_i = place("gate_i", [P, 2, SEQ], F32, g)
        next_at = shared + 2 * FT * SEQ * 4 - 2 * KT * SEQ * 4
        assert a[0] <= next_at
        a = [b[0] + 4 * 4 * P]
        emb = place("emb", [P, KT, SEQ], F32, a)
        assert a[0] <= next_at
        a = [next_at]
        next_hi = place("next_hi", [P, KT, SEQ], F32R, a)
        next_lo = place("next_lo", [P, KT, SEQ], F32R, a)

        banks = [ctx.enter_context(nc.psum_tensor(f"bank{n}", [P, SEQ], F32)) for n in range(8)]
        c_dram = nc.dram_tensor("forget_rows", (HEADS, SEQ), F32, kind="Internal").ap()

        unit_loaded = [sem(f"unit_loaded{s}") for s in range(SLOTS)]
        unit_split = sem("unit_split")
        unit_used = sem("unit_used")
        inputs_loaded = sem("inputs_loaded")
        consts_set = sem("consts_set")
        x_hi_ready, x_lo_ready = sem("x_hi_ready"), sem("x_lo_ready")
        mix_hi_ready, mix_lo_ready = sem("mix_hi_ready"), sem("mix_lo_ready")
        fg_done, fg_abs, fg_exp, fg_rows = sem("fg_done"), sem("fg_abs"), sem("fg_exp"), sem("fg_rows")
        fg_stored, row_loaded = sem("fg_stored"), sem("row_loaded")
        q_read, kv_read = sem("q_read"), sem("kv_read")
        vt_done, vt_read = sem("vt_done"), sem("vt_read")
        s_done, max_ready, exp_ready, probs_ready = (sem("s_done"), sem("max_ready"), sem("exp_ready"),
                                                     sem("probs_ready"))
        pt_done, pt_read, pv_done = sem("pt_done"), sem("pt_read"), sem("pv_done")
        o_read = sem("o_read")
        tile_read = {n: sem(f"{n}_read") for n in phases if n not in ("qkv", "rg")}
        part_sum, shift_done, shift_ready, parts_ready, sum_ready, mean_done, var_done, var_ready = (
            sem(n) for n in ("part_sum", "shift_done", "shift_ready", "parts_ready", "sum_ready", "mean_done",
                             "var_done", "var_ready"))
        dev_ready, diag_ready, spread_done, scaled = (
            sem(n) for n in ("dev_ready", "diag_ready", "spread_done", "scaled"))
        dist_ready, square_done = sem("dist_ready"), sem("square_done")
        x_ready, conv_first, conv_done, gelu_done, h_ready, h_hi_ready, h_lo_ready = (
            sem(n) for n in ("x_ready", "conv_first", "conv_done", "gelu_done", "h_ready", "h_hi_ready",
                             "h_lo_ready"))
        p_loaded, p_hi_ready, p_lo_ready, gated, emb_added = (
            sem(n) for n in ("p_loaded", "p_hi_ready", "p_lo_ready", "gated", "emb_added"))
        lru_w_loaded = [sem(f"lru_w_loaded{n}") for n in range(2)]
        lam_exp, lam_abs = sem("lam_exp"), sem("lam_abs")
        rg_first, rg_conv, rg_gates, rg_sig, rg_sqrt, rg_gelu, rg_y = (
            sem(n) for n in ("rg_first", "rg_conv", "rg_gates", "rg_sig", "rg_sqrt", "rg_gelu", "rg_y"))
        rg_x_read, rg_g_read, emb_done = sem("rg_x_read"), sem("rg_g_read"), sem("emb_done")
        stored = sem("stored")

        block = ctx.enter_context(nc.Block())

        def tail(widths, r):
            return sum(widths[:r % 3])

        def one(t, m):
            return t[:, m, :] if isinstance(m, int) else t[:, bass.ds(m, 1), :].rearrange("p a n -> p (a n)")

        def next_tiles(r):
            return ((), (0,), (1,), (2, 3))[r]

        @block.sync
        def _(sp):
            sp.dma_start(x[:], xT).then_inc(inputs_loaded, 16)
            sp.dma_start(cols[:], columns).then_inc(inputs_loaded, 16)
            sp.dma_start(wf[:], w_forget).then_inc(inputs_loaded, 16)
            sp.dma_start(bf[:], b_forget).then_inc(inputs_loaded, 16)
            square_first = [0]
            for name, ph in phases.items():
                base = square_first[0]
                n = len(ph.slots)
                with sp.Fori(0, ph.iters) as i:
                    for r, s in enumerate(ph.slots):
                        sp.wait_ge(unit_split, ph.slot_free(i, r))
                        w = ph.widths[r]
                        if name.startswith("down"):
                            c = tail(ph.widths, r)
                            src = w_down[bass.ds(i * (n // 3) + (int(name[-1]) * KT + r // 3), 1), :, c:c + w]
                        else:
                            src = w_square[bass.ds(i * n + (base + r), 1), :, :]
                        sp.dma_start(stage[:, s, 0:w],
                                     src.rearrange("a p n -> (a p) n")).then_inc(unit_loaded[s], 16)
                    if name == "rg":
                        for half in range(2):
                            sp.wait_ge(rg_gates, i * 2 + (half + 1))
                            sp.dma_start(w_ai[:, half, :], w_lru[bass.ds(i * 2 + half, 1), :, :]
                                         .rearrange("a p n -> (a p) n")).then_inc(lru_w_loaded[half], 16)
                if not name.startswith("down"):
                    square_first[0] += ph.iters * n
            for m in range(KT):
                sp.wait_ge(emb_added, 4 + KT + m + 1)
                sp.dma_start(outT[m], x[:, m, :]).then_inc(stored, 16)
            sp.wait_ge(stored, 16 * KT)

        @block.gpsimd
        def _(pool):
            pool.sem_inc(unit_split, SLOTS)
            pool.memset(waiter[:], 0.0)
            pool.memset(shift_of[:], 1.0 / (SHIFT_TILES * P))
            pool.memset(mean_of[:], 1.0 / D_MODEL)
            pool.memset(less_shift[:], -1.0 / P)
            pool.memset(ident[:], 1.0)
            pool.memset(ident_bf[:], 1.0)
            pool.memset(mask_bf[:], 0.0)
            pool.drain()
            pool.memset(q_ext[HEAD_DIM:HEAD_DIM + 1, :, :], 1.0)
            pool.drain()
            for m in (ident, ident_bf):
                pool.affine_select(out=m[:], in_=m[:], compare_op=ALU.is_equal, fill=0.0, base=0,
                                   pattern=[[-1, P]], channel_multiplier=1)
            pool.affine_select(out=mask_bf[:], in_=mask_bf[:], compare_op=ALU.is_ge, fill=MASKED, base=0,
                               pattern=[[-1, P]], channel_multiplier=1)
            pool.drain()
            pool.sem_inc(consts_set, 1)
            for ph in phases.values():
                with pool.Fori(0, ph.iters) as i:
                    for r, s in enumerate(ph.slots):
                        w = ph.widths[r]
                        pool.wait_ge(unit_loaded[s], ph.fills(i, r) * 16)
                        pool.wait_ge(unit_used, ph.slot_free(i, r))
                        pool.tensor_tensor(waiter[:], waiter[:], waiter[:], ALU.mult)
                        pool.drain()
                        pool.tensor_scalar(w_hi[:, s, 0:w], stage[:, s, 0:w], 1.0, 0.0, ALU.mult, ALU.add)
                        pool.drain()
                        pool.tensor_tensor(w_lo[:, s, 0:w], stage[:, s, 0:w], w_hi[:, s, 0:w].bitcast(F32),
                                           ALU.subtract).then_inc(unit_split, 1)

        @block.tensor
        def _(pe):
            pe.sem_inc(unit_used, SLOTS)

            def unit_ready(ph, i, r):
                pe.wait_ge(unit_split, ph.done(i, r))

            def three(out, s, c, m_hi, m_lo, first, last):
                pe.matmul(out, w_hi[:, s, c:c + P], m_hi, start=first, stop=False)
                pe.matmul(out, w_hi[:, s, c:c + P], m_lo, start=False, stop=False)
                return pe.matmul(out, w_lo[:, s, c:c + P], m_hi, start=False, stop=last)

            def whole_tile(ph, i, r, bank, hi, lo, beside={}):
                unit_ready(ph, i, r)
                for k in range(KT):
                    if k - 1 in beside:
                        beside[k - 1]()
                    mm = three(banks[bank][:], ph.slots[r], k * P, hi[:, k, :], lo[:, k, :], k == 0, k == KT - 1)
                mm.then_inc(unit_used, 1)

            def norm_shift(n):
                pe.wait_ge(part_sum, n + 1)
                pe.matmul(banks[6][:], shift_of[:], part_total[:], start=True, stop=True).then_inc(shift_done, 1)

            def token_sums(c, src, weights, start, stop):
                for t in range(QT):
                    mm = pe.matmul(banks[6][:, c + t:c + t + 1], src[:, t * P:(t + 1) * P], weights,
                                   start=start and t == 0, stop=stop, skip_group_check=True)
                return mm

            def norm_parts(n, step):
                if step == 0:
                    pe.wait_ge(parts_ready, n + 1)
                    pe.matmul(banks[7][:], mean_of[:], total[:], start=True, stop=False)
                    token_sums(0, shift, less_shift[:], True, False)
                if step == 1:
                    token_sums(0, total, mean_of[:, 0:1], False, False)
                if step == 2:
                    token_sums(QT, squares, mean_of[:, 0:1], False, False)

            def norm_sums(n):
                pe.wait_ge(sum_ready, n + 1)
                pe.matmul(banks[7][:], mean_of[:], x[:, KT - 1, :], start=False, stop=True).then_inc(mean_done, 1)
                token_sums(0, x[:, KT - 1, :], mean_of[:, 0:1], False, True)
                pe.wait_ge(square_done, (n + 1) * KT)
                token_sums(QT, dist[:, (KT - 1) % 2, :], mean_of[:, 0:1], False, True).then_inc(var_done, 1)

            def norm_spread(n):
                for t in range(QT):
                    pe.wait_ge(diag_ready, n * QT + t + 1)
                    mm = pe.matmul(banks[6][:, t * P:(t + 1) * P], mean_of[:], dist[:, 0, t * P:(t + 1) * P],
                                   start=True, stop=True, skip_group_check=True)
                mm.then_inc(spread_done, 1)

            pe.wait_ge(inputs_loaded, 64)
            pe.wait_ge(consts_set, 1)
            for k in range(KT):
                mm = pe.matmul(banks[0][0:HEADS, :], wf[:, k, :], x[:, k, :], start=(k == 0), stop=(k == KT - 1))
            mm.then_inc(fg_done, 1)

            qkv = phases["qkv"]
            S_AT = [(3, 384), (4, 0), (3, 0), (2, 0)]

            def project(j, r, bank, beside={}):
                whole_tile(qkv, j, r, bank, x_hi, x_lo, beside)

            def scores(j, h):
                pe.wait_ge(exp_ready, j * 8 + (h * 4))
                if h == 0:
                    pe.wait_ge(q_read, j + 1)
                    pe.wait_ge(kv_read, j * 2 + 2)
                    pe.wait_ge(row_loaded, j * 16 + 16)
                for t in (3, 2, 0, 1):
                    bank, c = S_AT[t]
                    w = (t + 1) * P
                    pe.matmul(banks[bank][:, c:c + w], q_ext[0:HEAD_DIM + 1, h, t * P:(t + 1) * P],
                              k_ext[0:HEAD_DIM + 1, h, 0:w], start=True, stop=False, skip_group_check=True)
                    mm = pe.matmul(banks[bank][:, c + w - P:c + w], ident_bf[:], mask_bf[:], start=False,
                                   stop=True, skip_group_check=True)
                mm.then_inc(s_done, 1)

            PT_AT = [(5, 0), (6, 0), (5, 0), (5, 256)]

            def turn_probs(j, h, step):
                if step == 0:
                    pe.wait_ge(probs_ready, j * 2 + (h + 1))
                pe.wait_ge(pt_read, j * 6 + (h * 3 + max(step, 1)))
                for kt in ((0,), (1,), (2, 3))[step]:
                    bank, c = PT_AT[kt]
                    for t in range(kt, QT):
                        a0 = (t * (t + 1) // 2 + kt) * P
                        mm = pe.transpose(banks[bank][:, c + (t - kt) * P:c + (t - kt + 1) * P],
                                          probs[:, h, a0:a0 + P], ident[:])
                mm.then_inc(pt_done, 1)

            def sum_values(j, h, tiles):
                if h == 0 and tiles[0] == 0:
                    pe.wait_ge(vt_read, j + 1)
                for kt in tiles:
                    w, c0 = (QT - kt) * P, sum(QT - t for t in range(kt)) * P
                    pe.wait_ge(pt_read, j * 6 + (h * 3 + min(kt, 2) + 2))
                    mm = pe.matmul(banks[7][h * HEAD_DIM:(h + 1) * HEAD_DIM, kt * P:SEQ],
                                   v_tok[:, kt, h * HEAD_DIM:(h + 1) * HEAD_DIM], probs_t[:, c0:c0 + w],
                                   start=(kt == 0), stop=(kt == QT - 1), skip_group_check=True)
                if tiles[-1] == QT - 1:
                    mm.then_inc(pv_done, 1)

            def turn_values(j):
                pe.wait_ge(kv_read, j * 2 + 2)
                pe.wait_ge(o_read, j + 1)
                for t in range(QT):
                    mm = pe.transpose(banks[7][:, t * P:(t + 1) * P], v_chan[:, t * P:(t + 1) * P], ident[:])
                mm.then_inc(vt_done, 1)

            def head(j, h, at):
                steps = (lambda: turn_probs(j, h, 0), lambda: turn_probs(j, h, 1),
                         lambda: turn_probs(j, h, 2), lambda: sum_values(j, h, (0, 1)),
                         lambda: sum_values(j, h, (2, 3)))
                beside = {}
                for k, step in zip(at, steps):
                    beside.setdefault(k, []).append(step)
                return {k: (lambda todo=todo: [step() for step in todo]) for k, todo in beside.items()}

            pe.wait_ge(x_lo_ready, KT)
            pe.wait_ge(fg_abs, 1)
            project(0, 0, 0)
            project(0, 1, 1)
            pe.wait_ge(q_read, 1)
            project(0, 2, 0)
            with pe.Fori(1, PAIRS) as j:
                scores(j - 1, 0)
                pe.wait_ge(kv_read, j * 2)
                project(j, 0, 0, {TURN_AT: lambda: turn_values(j - 1)})
                scores(j - 1, 1)
                project(j, 1, 1, head(j - 1, 0, FIRST_AT))
                pe.wait_ge(q_read, j + 1)
                project(j, 2, 0, head(j - 1, 1, SECOND_AT))
            EARLY_OUT = [(k, r) for r in range(3) for k in range(KT - 1)]

            def early_out(r, beside):
                unit_ready(phases["out0"], 0, r)
                for k, _ in EARLY_OUT[:KT - 1]:
                    if r == 0:
                        pe.wait_ge(mix_lo_ready, k + 1)
                    three(banks[r][:], phases["out0"].slots[r], k * P, mix_hi[:, k, :], mix_lo[:, k, :],
                          k == 0, False)
                    if k in beside:
                        beside[k]()

            scores(PAIRS - 1, 0)
            pe.wait_ge(kv_read, PAIRS * 2)
            early_out(0, {TURN_AT: lambda: turn_values(PAIRS - 1)})
            scores(PAIRS - 1, 1)
            early_out(1, head(PAIRS - 1, 0, FIRST_AT))
            pe.wait_ge(exp_ready, PAIRS * 8)
            early_out(2, head(PAIRS - 1, 1, SECOND_AT))

            def square_phase(name, hi, lo, ready, count, together, wide, between=None, bank_free=None, started=(),
                             beside_last={}):
                ph = phases[name]
                steps = [(k, r) for k in range(together) for r in range(wide)]
                steps += [(k, r) for r in range(wide, 4) for k in range(together)]
                steps += [(k, r) for r in range(4) for k in range(together, KT)]
                steps = [step for step in steps if step not in started]
                waited = set()
                for k, r in steps:
                    if k == 0:
                        unit_ready(ph, 0, r)
                        pe.wait_ge(tile_read[name], r + 1)
                        if bank_free is not None:
                            bank_free(r)
                    if k not in waited:
                        waited.add(k)
                        pe.wait_ge(ready, count + k + 1)
                    mm = three(banks[r][:], ph.slots[r], k * P, hi[:, k, :], lo[:, k, :], k == 0, k == KT - 1)
                    if k == KT - 1:
                        mm.then_inc(unit_used, 1)
                if between is not None:
                    between()
                with pe.Fori(1, ph.iters) as i:
                    for r in range(4):
                        pe.wait_ge(tile_read[name], i * 4 + (r + 1))
                        whole_tile(ph, i, r, r, hi, lo, beside_last if r == 3 else {})

            def down_tile(name, layer, i, half, beside={}):
                ph = phases[name]
                pe.wait_ge(tile_read[name], i * 2 + (half + 1))
                k = 0
                for part in range(3):
                    r = half * 3 + part
                    unit_ready(ph, i, r)
                    for c in range(ph.widths[r] // P):
                        if k >= FT - 4:
                            pe.wait_ge(h_lo_ready, layer * FT + 2 + k + 1)
                        if k - 1 in beside:
                            beside[k - 1]()
                        mm = three(banks[half][:], ph.slots[r], c * P, h_hi[:, k, :], h_lo[:, k, :],
                                   k == 0, k == FT - 1)
                        k += 1
                    mm.then_inc(unit_used, 1)

            def down_rounds(name, layer, a, b):
                with pe.Fori(a, b) as i:
                    for half in range(2):
                        down_tile(name, layer, i, half)

            def ple_tiles(name, layer, a, b):
                ph = phases[name]
                for m in range(a, b):
                    r, c = m // 4, m % 4
                    if c == 0:
                        unit_ready(ph, 0, r)
                    pe.wait_ge(p_lo_ready, (layer + 1) * 2)
                    if m >= 4:
                        pe.wait_ge(tile_read[name], m - 3)
                    for k in range(2):
                        mm = three(banks[2 + m % 4][:], ph.slots[r], (c * 2 + k) * P, p_hi[:, k, :], p_lo[:, k, :],
                                   k == 0, k == 1)
                    mm.then_inc(emb_done, 1)
                    if c == 3:
                        pe.wait_ge(emb_done, layer * KT + m + 1)
                        pe.sem_inc(unit_used, 1)
                if b == KT:
                    pe.wait_ge(tile_read[name], KT - 2)

            def rest_of_layer(layer):
                square_phase(f"out{layer}", mix_hi, mix_lo, mix_lo_ready, layer * KT,
                             OUT_TOGETHER[layer], 4, lambda: norm_shift(2 * layer), rg_bank_free if layer else None, () if layer else EARLY_OUT,
                             {PARTS_AT + step: (lambda step=step: norm_parts(2 * layer, step)) for step in range(3)})
                norm_sums(2 * layer)
                norm_spread(2 * layer)
                square_phase(f"up{layer}", x_hi, x_lo, x_lo_ready, (layer * 3 + 1) * KT, KT, 3)
                pe.wait_ge(tile_read[f"up{layer}"], 4 + 2 * FT - 2)
                down_rounds(f"down{layer}", layer, 0, KT // 4)
                norm_shift(2 * layer + 1)
                down_rounds(f"down{layer}", layer, KT // 4, KT // 2 - 1)
                down_tile(f"down{layer}", layer, KT // 2 - 1, 0)
                down_tile(f"down{layer}", layer, KT // 2 - 1, 1, 
                          {2 * KT - 4 + 2 * step: (lambda step=step: norm_parts(2 * layer + 1, step)) for step in range(3)})
                ple_tiles(f"ple{layer}", layer, 0, PLE_AT[0])
                norm_sums(2 * layer + 1)
                ple_tiles(f"ple{layer}", layer, PLE_AT[0], PLE_AT[1])
                norm_spread(2 * layer + 1)
                ple_tiles(f"ple{layer}", layer, PLE_AT[1], KT)
                square_phase(f"gate{layer}", x_hi, x_lo, x_lo_ready, (layer * 3 + 2) * KT, KT, 3)

            def rg_bank_free(r):
                pe.wait_ge((rg_x_read, rg_g_read)[r // 2], KT + 1 + r % 2)

            rest_of_layer(0)

            rg = phases["rg"]
            pe.sem_inc(rg_gates, 2)

            def rg_gate_products(i, half):
                pe.wait_ge(rg_conv, i * 2 + (half + 1))
                pe.wait_ge(lru_w_loaded[half], (i + 1) * 16)
                pe.wait_ge(rg_sig, i * 2 + (half + 1))
                pe.matmul(banks[4 + half * 2][:], w_ai[:, half, 0:P], conv_x[:, half, :], start=True, stop=True)
                pe.matmul(banks[5 + half * 2][:], w_ai[:, half, P:2 * P], conv_x[:, half, :], start=True,
                          stop=True).then_inc(rg_gates, 1)

            def rg_round(i, first):
                for r in range(4):
                    if first:
                        pe.wait_ge(tile_read["gate0"], 4 + KT - 3 + r)
                    if r == 0 and first:
                        pe.wait_ge(x_lo_ready, 3 * KT + 1)
                    pe.wait_ge((rg_x_read, rg_g_read)[r // 2], i * 2 + (r % 2 + 1))
                    whole_tile(rg, i, r, r, next_hi, next_lo,
                               {k: (lambda k=k: pe.wait_ge(x_lo_ready, 3 * KT + k + 2)) for k in range(KT - 1)}
                               if first and r == 0 else {})
                    if r == 2:
                        rg_gate_products(i, 0)
                        rg_gate_products(i, 1)

            rg_round(0, True)
            with pe.Fori(1, rg.iters) as i:
                rg_round(i, False)
            rest_of_layer(1)

        @block.vector
        def _(dve):
            def log1p_twice(q, e, den, q2, acc):
                dve.tensor_scalar(den, e, 2.0, None, ALU.add)
                dve.drain()
                dve.reciprocal(q2, den)
                dve.drain()
                dve.tensor_tensor(q, e, q2, ALU.mult)
                dve.drain()
                dve.tensor_tensor(q2, q, q, ALU.mult)
                dve.drain()
                dve.tensor_scalar(acc, q2, LOG1P_TERMS[-1], None, ALU.mult)
                dve.drain()
                for c in LOG1P_TERMS[-2:0:-1]:
                    dve.scalar_tensor_tensor(acc, acc, c, q2, ALU.add, ALU.mult)
                    dve.drain()
                dve.scalar_tensor_tensor(acc, acc, LOG1P_TERMS[0], q, ALU.add, ALU.mult)
                dve.drain()

            def norm_tile(n, m):
                xm = x[:, m, :]
                dve.tensor_tensor(dist[:, m % 2, :], xm, shift[:], ALU.subtract).then_inc(dist_ready, 1)

            def layer_norm(n, layer, g):
                def center(m):
                    dve.tensor_tensor(x[:, m, :], x[:, m, :], banks[7][:], ALU.subtract)

                dve.wait_ge(mean_done, n + 1)
                center(0)
                center(1)
                dve.wait_ge(var_done, n + 1)
                dve.tensor_copy(norm_stat[:, 0:QT], banks[6][:, 0:QT])
                dve.drain()
                dve.tensor_tensor(norm_stat[:, 0:QT], banks[6][:, 0:QT], norm_stat[:, 0:QT], ALU.mult)
                dve.drain()
                dve.tensor_tensor(norm_stat[:, QT:2 * QT], banks[6][:, QT:2 * QT], norm_stat[:, 0:QT],
                                  ALU.subtract).then_inc(var_ready, 1)
                center(2)
                dve.wait_ge(dev_ready, n + 1)
                dve.reciprocal(norm_stat[:, 0:QT], norm_stat[:, QT:2 * QT])
                dve.drain()
                for t in range(QT):
                    dve.tensor_scalar(dist[:, 0, t * P:(t + 1) * P], ident[:], norm_stat[:, t:t + 1],
                                      float(D_MODEL), ALU.mult, ALU.mult).then_inc(diag_ready, 1)
                center(3)
                dve.drain()
                dve.wait_ge(spread_done, n + 1)
                for m in range(KT + 1):
                    if m < KT:
                        c = COLS[g, layer] + m
                        dve.scalar_tensor_tensor(x[:, m, :], x[:, m, :], cols[:, c:c + 1], banks[6][:],
                                                 ALU.mult, ALU.mult).then_inc(scaled, 1)
                    if m + 4 < KT:
                        center(m + 4)
                    if m > 0:
                        dve.wait_ge(x_hi_ready, (x_round[0] * KT) + m)
                        dve.tensor_tensor(x_lo[:, m - 1, :], x[:, m - 1, :], x_hi[:, m - 1, :].bitcast(F32),
                                          ALU.subtract).then_inc(x_lo_ready, 1)
                    dve.drain()
                x_round[0] += 1

            x_round = [0]

            def residual_phase(name, n, per_round, units):
                ph = phases[name]

                def residual(i, r, add_from, add_to):
                    dve.wait_ge(unit_used, ph.done(i, (r + 1) * units - 1))
                    xm = x[:, bass.ds(i * per_round + r, 1), :].rearrange("p a n -> p (a n)") \
                        if not isinstance(i, int) else x[:, i * per_round + r, :]
                    dve.scalar_tensor_tensor(xm, xm, ALPHA, banks[r][:], ALU.mult,
                                             ALU.add).then_inc(tile_read[name], 1)
                    dve.drain()
                    if add_from is not None:
                        dve.tensor_tensor(add_to, add_from, xm, ALU.add)

                def add_square(m, first):
                    dve.wait_ge(square_done, n * KT + m + 1)
                    if first:
                        dve.tensor_copy(squares[:], dist[:, 0, :])
                    else:
                        dve.tensor_tensor(squares[:], squares[:], dist[:, m % 2, :], ALU.add)
                    dve.drain()

                tiles = [(m // per_round, m % per_round) for m in range(KT)]
                residual(*tiles[0], None, None)
                residual(*tiles[1], x[:, 0, :], part_total[:])
                residual(*tiles[2], part_total[:], part_total[:])
                dve.drain()
                dve.sem_inc(part_sum, 1)
                residual(*tiles[3], part_total[:], total[:])
                dve.wait_ge(shift_ready, n + 1)
                for m in range(KT):
                    if m == KT - 1:
                        add_square(m - 1, False)
                        dve.sem_inc(parts_ready, 1)
                        residual(*tiles[m], None, None)
                        dve.sem_inc(sum_ready, 1)
                    elif m >= 4:
                        residual(*tiles[m], total[:], total[:])
                    norm_tile(n, m)
                    if 0 < m < KT - 1:
                        add_square(m - 1, m == 1)

            dve.wait_ge(inputs_loaded, 64)
            for m in range(KT):
                dve.wait_ge(x_hi_ready, m + 1)
                dve.tensor_tensor(x_lo[:, m, :], x[:, m, :], x_hi[:, m, :].bitcast(F32),
                                  ALU.subtract).then_inc(x_lo_ready, 1)
            x_round[0] = 1

            dve.wait_ge(fg_done, 1)
            z, e, r0, r1 = (fg[:, n, :] for n in range(4))
            dve.tensor_scalar(z, banks[0][0:HEADS, :], bf[:, 0:1], None, ALU.add)
            dve.drain()
            dve.scalar_tensor_tensor(e, z, -1.0, z, ALU.mult, ALU.max).then_inc(fg_abs, 1)
            dve.wait_ge(fg_exp, 1)
            log1p_twice(r0, e, r1, r1, total[0:HEADS, :])
            dve.tensor_scalar(z, z, -1.0, 0.0, ALU.mult, ALU.max)
            dve.memset(r0, 1.0)
            dve.drain()
            dve.scalar_tensor_tensor(e, total[0:HEADS, :], 2.0, z, ALU.mult, ALU.add)
            dve.drain()
            dve.tensor_tensor_scan(r1, r0, e, 0.0, ALU.mult, ALU.add).then_inc(fg_rows, 1)

            def queries(j):
                dve.wait_ge(unit_used, phases["qkv"].done(j, 0))
                dve.wait_ge(s_done, j * 2)
                for h in range(2):
                    dve.tensor_scalar(q_ext[0:HEAD_DIM, h, :], banks[0][h * HEAD_DIM:(h + 1) * HEAD_DIM, :],
                                      HEAD_DIM ** -0.5, None, ALU.mult)
                dve.drain()
                dve.sem_inc(q_read, 1)

            def maxima(j, h):
                dve.wait_ge(s_done, j * 2 + (h + 1))
                for t, (bank, c) in ((3, (2, 0)), (2, (3, 0)), (0, (3, 384)), (1, (4, 0))):
                    mx = dve.tensor_reduce(stat[:, h, t:t + 1], banks[bank][:, c:c + (t + 1) * P], AX_X, ALU.max,
                                           negate=True)
                    mx.then_inc(max_ready, 1)

            def normalise(j, h):
                dve.wait_ge(exp_ready, j * 8 + (h * 4 + 4))
                dve.reciprocal(stat[:, h, 8:12], stat[:, h, 4:8])
                dve.drain()
                for t in range(QT):
                    a0, w = t * (t + 1) // 2 * P, (t + 1) * P
                    nm = dve.tensor_scalar(probs[:, h, a0:a0 + w], probs[:, h, a0:a0 + w],
                                           stat[:, h, 8 + t:9 + t], None, ALU.mult)
                dve.drain()
                dve.sem_inc(probs_ready, 1)

            def mixed(j):
                dve.wait_ge(mix_hi_ready, j + 1)
                lo = mix_lo[:, bass.ds(j, 1), :].rearrange("p a n -> p (a n)")
                hi = mix_hi[:, bass.ds(j, 1), :].rearrange("p a n -> p (a n)")
                dve.tensor_tensor(lo, banks[7][:], hi.bitcast(F32), ALU.subtract)
                dve.drain()
                dve.sem_inc(mix_lo_ready, 1)
                dve.sem_inc(o_read, 1)

            dve.sem_inc(o_read, 1)
            dve.wait_ge(unit_used, phases["qkv"].done(0, 0))
            for h in range(2):
                dve.tensor_scalar(q_ext[0:HEAD_DIM, h, :], banks[0][h * HEAD_DIM:(h + 1) * HEAD_DIM, :],
                                  HEAD_DIM ** -0.5, None, ALU.mult)
            dve.drain()
            dve.sem_inc(q_read, 1)
            with dve.Fori(1, PAIRS) as j:
                maxima(j - 1, 0)
                normalise(j - 1, 0)
                maxima(j - 1, 1)
                normalise(j - 1, 1)
                queries(j)
                dve.wait_ge(pv_done, j * 2)
                mixed(j - 1)
            maxima(PAIRS - 1, 0)
            normalise(PAIRS - 1, 0)
            maxima(PAIRS - 1, 1)
            normalise(PAIRS - 1, 1)
            mixed(PAIRS - 1)

            def conv_ffn(layer):
                name = f"up{layer}"
                base = COLS["conv", layer]
                with dve.Fori(0, FT // 2) as i:
                    for half in range(2):
                        for part in (1, 0):
                            r = half * 2 + part
                            c = (i * 4 + r) * (CONV_F + 1) + base
                            t = tmp[:, r, :]
                            dve.wait_ge(conv_first, layer * 2 * FT + i * 4 + (half * 2 + (2 - part)))
                            dve.scalar_tensor_tensor(t[:, 1:SEQ], banks[r][:, 0:SEQ - 1], cols[:, bass.ds(c + 1, 1)],
                                                     t[:, 1:SEQ], ALU.mult, ALU.add)
                            dve.drain()
                            dve.scalar_tensor_tensor(t[:, 2:SEQ], banks[r][:, 0:SEQ - 2], cols[:, bass.ds(c, 1)],
                                                     t[:, 2:SEQ], ALU.mult, ALU.add).then_inc(conv_done, 1)
                            dve.wait_ge(conv_done, layer * 2 * FT + i * 4 + (half * 2 + (2 - part)))
                        dve.sem_inc(tile_read[name], 2)
                        n = layer * FT + i * 2 + (half + 1)
                        dve.wait_ge(gelu_done, n)
                        dve.tensor_tensor(tmp[:, half * 2, :], tmp[:, half * 2, :], tmp[:, half * 2 + 1, :],
                                          ALU.mult).then_inc(h_ready, 1)
                        dve.wait_ge(h_hi_ready, n)
                        lo = h_lo[:, bass.ds(i * 2 + half, 1), :].rearrange("p a n -> p (a n)")
                        hi = h_hi[:, bass.ds(i * 2 + half, 1), :].rearrange("p a n -> p (a n)")
                        dve.tensor_tensor(lo, tmp[:, half * 2, :], hi.bitcast(F32), ALU.subtract)\
                            .then_inc(h_lo_ready, 1)

            def embed(layer):
                for k in range(2):
                    dve.wait_ge(p_hi_ready, layer * 2 + k + 1)
                    dve.tensor_tensor(p_lo[:, k, :], p_in[:, k, :], p_hi[:, k, :].bitcast(F32),
                                      ALU.subtract).then_inc(p_lo_ready, 1)

            def gate(layer):
                last = layer == DEPTH - 1
                with dve.Fori(0, 2) as i:
                    for r in range(4):
                        m = i * 4 + r
                        xm = x[:, bass.ds(m, 1), :].rearrange("p a n -> p (a n)")
                        dve.wait_ge(gated, i * 4 + (layer * KT + r + 1))
                        dve.tensor_tensor(tmp[:, r, :], tmp[:, r, :],
                                          emb[:, bass.ds(m, 1), :].rearrange("p a n -> p (a n)"), ALU.mult)
                        dve.drain()
                        dve.tensor_tensor(xm, xm, tmp[:, r, :], ALU.add).then_inc(emb_added, 1)
                        dve.drain()
                        if not last:
                            for m in next_tiles(r):
                                dve.wait_ge(x_hi_ready, i * 4 + (x_round[0] * KT + m + 1))
                                dve.tensor_tensor(one(next_lo, i * 4 + m), one(x, i * 4 + m),
                                                  one(next_hi, i * 4 + m).bitcast(F32),
                                                  ALU.subtract).then_inc(x_lo_ready, 1)
                x_round[0] += not last

            def rest_of_layer(layer):
                residual_phase(f"out{layer}", 2 * layer, 4, 1)
                dve.sem_inc(tile_read[f"up{layer}"], 4)
                layer_norm(2 * layer, layer, "ln1_g")
                dve.sem_inc(tile_read[f"down{layer}"], 2)
                conv_ffn(layer)
                embed(layer)
                residual_phase(f"down{layer}", 2 * layer + 1, 2, 3)
                layer_norm(2 * layer + 1, layer, "ln2_g")
                gate(layer)

            lz, le, l0, l1, l2 = (lam4[:, n, :] for n in range(5))
            c = COLS["rg_lam"]
            dve.drain()
            dve.tensor_scalar(lz, cols[:, c:c + KT], -1.0, None, ALU.mult)
            dve.drain()
            dve.tensor_tensor(le, lz, cols[:, c:c + KT], ALU.max).then_inc(lam_abs, 1)
            dve.wait_ge(lam_exp, 1)
            log1p_twice(l0, le, l1, l1, l2)
            dve.tensor_scalar(lz, lz, 0.0, 4.0, ALU.max, ALU.mult)
            dve.drain()
            dve.scalar_tensor_tensor(lam4[:, 5, :], l2, 8.0, lz, ALU.mult, ALU.add)
            dve.drain()
            dve.tensor_scalar(lz, lam4[:, 5, :], -2.0, None, ALU.mult).then_inc(lam_abs, 1)

            dve.sem_inc(h_lo_ready, 2)
            dve.sem_inc(emb_added, 4)
            for layer in range(DEPTH):
                dve.sem_inc(tile_read[f"out{layer}"], 4)
            rest_of_layer(0)

            dve.sem_inc(rg_x_read, 2)

            def rg_convolve(i, half):
                c = (i * 2 + half) * (CONV_B + 1) + COLS["rg_conv"]
                dve.wait_ge(rg_first, i * 2 + (half + 1))
                for lag in range(1, CONV_B):
                    dve.scalar_tensor_tensor(conv_x[:, half, lag:SEQ], banks[half][:, 0:SEQ - lag],
                                             cols[:, bass.ds(c + (CONV_B - 1 - lag), 1)],
                                             conv_x[:, half, lag:SEQ], ALU.mult, ALU.add)
                    dve.drain()
                dve.sem_inc(rg_x_read, 1)
                dve.sem_inc(rg_conv, 1)

            def rg_input(i, half):
                dve.wait_ge(rg_sig, i * 2 + (half + 3))
                dve.tensor_tensor(gate_i[:, half, :], gate_i[:, half, :], conv_x[:, half, :], ALU.mult)

            def rg_scan(i, half):
                dve.wait_ge(rg_sqrt, i * 2 + (half + 1))
                dve.scalar_tensor_tensor(drive[:], decay[:, half, :], 1.0, half_t[:, half, :], ALU.add, ALU.mult)
                dve.drain()
                dve.tensor_tensor(drive[:], drive[:], gate_i[:, half, :], ALU.mult)
                dve.drain()
                dve.tensor_tensor_scan(state[:, half, :], decay[:, half, :], drive[:], 0.0, ALU.mult, ALU.add)
                dve.drain()

            def rg_output(i, half):
                dve.wait_ge(rg_gelu, i * 2 + (half + 1))
                dve.tensor_tensor(state[:, half, :], state[:, half, :], gelu_g[:, half, :],
                                  ALU.mult).then_inc(rg_y, 1)

            def rg_low(i, half):
                dve.wait_ge(mix_hi_ready, i * 2 + (half + 1 + KT))
                m = i * 2 + half
                dve.tensor_tensor(one(mix_lo, m), state[:, half, :], one(mix_hi, m).bitcast(F32),
                                  ALU.subtract).then_inc(mix_lo_ready, 1)

            with dve.Fori(0, KT // 2) as i:
                for step in (rg_convolve, rg_input, rg_scan, rg_output, rg_low):
                    for half in range(2):
                        step(i, half)
            rest_of_layer(1)

        @block.scalar
        def _(act):
            x_round = [0]

            def norm_squares(n):
                act.wait_ge(shift_done, n + 1)
                act.copy(shift[:], banks[6][:]).then_inc(shift_ready, 1)
                for m in range(KT):
                    act.wait_ge(dist_ready, n * KT + m + 1)
                    act.activation(dist[:, m % 2, :], dist[:, m % 2, :], ACT.Square).then_inc(square_done, 1)

            def layer_norm(n, layer, b, beside=None):
                act.wait_ge(var_ready, n + 1)
                act.activation(norm_stat[:, QT:2 * QT], norm_stat[:, QT:2 * QT], ACT.Sqrt,
                               bias=LN_EPS).then_inc(dev_ready, 1)
                if beside is not None:
                    beside(-1)
                for m in range(KT):
                    c = COLS[b, layer] + m
                    act.wait_ge(scaled, n * KT + m + 1)
                    act.activation(x_hi[:, m, :], x[:, m, :], ACT.Identity, bias=cols[:, c:c + 1])
                    act.activation(x[:, m, :], x[:, m, :], ACT.Identity,
                                   bias=cols[:, c:c + 1]).then_inc(x_hi_ready, 1)
                    if beside is not None:
                        beside(m)

            act.wait_ge(inputs_loaded, 64)
            for m in range(KT):
                act.copy(x_hi[:, m, :], x[:, m, :]).then_inc(x_hi_ready, 1)

            act.wait_ge(fg_abs, 1)
            act.activation(fg[:, 1, :], fg[:, 1, :], ACT.Exp, scale=-1.0).then_inc(fg_exp, 1)
            act.wait_ge(fg_rows, 1)
            act.dma_start(c_dram, fg[:, 3, :]).then_inc(fg_stored, 16)
            act.wait_ge(fg_stored, 16)

            def keys(j, scored):
                act.wait_ge(unit_used, phases["qkv"].done(j, 1))
                if scored:
                    act.wait_ge(s_done, j * 2)
                act.dma_start(k_ext[HEAD_DIM:HEAD_DIM + 1, :, :],
                              c_dram.rearrange("(j h) n -> j h n", h=2)[bass.ds(j, 1), :, :]).then_inc(row_loaded, 16)
                for h in range(2):
                    act.copy(k_ext[0:HEAD_DIM, h, :], banks[1][h * HEAD_DIM:(h + 1) * HEAD_DIM, :])
                act.drain()
                act.sem_inc(kv_read, 1)

            def values(j, turned):
                act.wait_ge(unit_used, phases["qkv"].done(j, 2))
                if turned:
                    act.wait_ge(vt_done, j)
                act.copy(v_chan[:], banks[0][:]).then_inc(kv_read, 1)

            def token_values(j):
                act.wait_ge(vt_done, j + 1)
                act.copy(v_tok[:].rearrange("p t c -> p (t c)"), banks[7][:]).then_inc(vt_read, 1)

            def exponentials(j, h, weighed):
                if weighed:
                    act.wait_ge(pt_done, j * 6 - (3 - h * 3))
                for n, (t, (bank, c)) in enumerate(((3, (2, 0)), (2, (3, 0)), (0, (3, 384)), (1, (4, 0)))):
                    act.wait_ge(max_ready, j * 8 + (h * 4 + max(n + 1, 3 if n in (1, 2) else 0)))
                    a0, w = t * (t + 1) // 2 * P, (t + 1) * P
                    act.activation(probs[:, h, a0:a0 + w], banks[bank][:, c:c + w], ACT.Exp,
                                   bias=stat[:, h, t:t + 1], accum_out=stat[:, h, 4 + t:5 + t])
                    act.drain()
                    act.sem_inc(exp_ready, 1)

            def turned_probs(j, h, weighed):
                for step, (bank, a0, w) in enumerate(((5, 0, 512), (6, 512, 384), (5, 896, 384))):
                    act.wait_ge(pt_done, j * 6 + (h * 3 + step + 1))
                    if step == 0 and weighed:
                        act.wait_ge(pv_done, j * 2 + h)
                    act.copy(probs_t[:, a0:a0 + w], banks[bank][:, 0:w]).then_inc(pt_read, 1)

            def outputs(j):
                act.wait_ge(pv_done, j * 2 + 2)
                act.copy(mix_hi[:, bass.ds(j, 1), :].rearrange("p a n -> p (a n)"), banks[7][:])\
                    .then_inc(mix_hi_ready, 1)

            def attend(j, j_next, project_it, first):
                exponentials(j, 0, not first)
                token_values(j)
                exponentials(j, 1, not first)
                turned_probs(j, 0, not first)
                if project_it:
                    keys(j_next, True)
                turned_probs(j, 1, True)
                outputs(j)
                if project_it:
                    values(j_next, True)

            act.sem_inc(pt_read, 1)
            keys(0, False)
            values(0, False)
            attend(0, 1, True, True)
            with act.Fori(2, PAIRS) as j:
                attend(j - 1, j, True, False)
            attend(PAIRS - 1, None, False, False)

            def conv_ffn(layer):
                name = f"up{layer}"
                base = COLS["conv", layer]
                with act.Fori(0, FT // 2) as i:
                    for half in range(2):
                        act.wait_ge(unit_used, phases[name].done(i, half * 2 + 1))
                        act.wait_ge(h_lo_ready, i * 2 + (layer * FT + half + 1))
                        for part in (1, 0):
                            r = half * 2 + part
                            c = (i * 4 + r) * (CONV_F + 1) + base
                            act.activation(tmp[:, r, :], banks[r][:], ACT.Identity, bias=cols[:, bass.ds(c + 3, 1)],
                                           scale=cols[:, bass.ds(c + 2, 1)]).then_inc(conv_first, 1)
                        act.wait_ge(conv_done, i * 4 + (layer * 2 * FT + half * 2 + 1))
                        act.activation(tmp[:, half * 2 + 1, :], tmp[:, half * 2 + 1, :],
                                       ACT.Gelu_apprx_tanh).then_inc(gelu_done, 1)
                        act.wait_ge(h_ready, i * 2 + (layer * FT + half + 1))
                        act.copy(h_hi[:, bass.ds(i * 2 + half, 1), :].rearrange("p a n -> p (a n)"),
                                 tmp[:, half * 2, :]).then_inc(h_hi_ready, 1)

            def embedding_input(layer):
                act.wait_ge(unit_used, phases[f"up{layer}"].done(2 * FT // 4 - 1, 3))
                act.wait_ge(h_lo_ready, layer * FT + 2 + FT)
                act.dma_start(p_in[:], pT[layer]).then_inc(p_loaded, 16)
                act.wait_ge(p_loaded, 16 * (layer + 1))
                for k in range(2):
                    act.copy(p_hi[:, k, :], p_in[:, k, :]).then_inc(p_hi_ready, 1)

            def embedding(layer, a, b):
                for m in range(a, b):
                    act.wait_ge(emb_done, layer * KT + m + 1)
                    act.copy(emb[:, m, :], banks[2 + m % 4][:]).then_inc(tile_read[f"ple{layer}"], 1)

            def gate(layer):
                name = f"gate{layer}"
                with act.Fori(0, 2) as i:
                    for r in range(4):
                        act.wait_ge(unit_used, phases[name].done(i, r))
                        act.wait_ge(emb_added, i * 4 + (layer * KT + r + 1))
                        act.activation(tmp[:, r, :], banks[r][:], ACT.Sigmoid,
                                       bias=cols[:, bass.ds(i * 4 + (COLS["gate_b", layer] + r), 1)])\
                            .then_inc(gated, 1)
                        act.drain()
                        act.sem_inc(tile_read[name], 1)
                        if layer < DEPTH - 1:
                            for m in next_tiles(r):
                                act.wait_ge(emb_added, i * 4 + (4 + layer * KT + m + 1))
                                act.copy(one(next_hi, i * 4 + m), one(x, i * 4 + m)).then_inc(x_hi_ready, 1)

            def rest_of_layer(layer):
                norm_squares(2 * layer)
                layer_norm(2 * layer, layer, "ln1_b")
                conv_ffn(layer)
                embedding_input(layer)
                norm_squares(2 * layer + 1)
                act.sem_inc(tile_read[f"gate{layer}"], 4)
                layer_norm(2 * layer + 1, layer, "ln2_b", 
                           lambda m: embedding(layer, EMB_READ[m + 1], EMB_READ[m + 2]))
                gate(layer)

            act.wait_ge(lam_abs, 1)
            act.activation(lam4[:, 1, :], lam4[:, 1, :], ACT.Exp, scale=-1.0).then_inc(lam_exp, 1)
            rest_of_layer(0)

            act.wait_ge(lam_abs, 2)
            act.sem_inc(rg_sig, 2)
            act.sem_inc(rg_g_read, 2)
            rg = phases["rg"]

            def col(c):
                return cols[:, c:c + 1] if isinstance(c, int) else cols[:, bass.ds(c, 1)]

            def rg_blocks(i, reused):
                if reused:
                    act.wait_ge(rg_y, i * 2)
                for half in range(2):
                    c = (i * 2 + half) * (CONV_B + 1) + COLS["rg_conv"]
                    act.wait_ge(unit_used, rg.done(i, half))
                    act.activation(conv_x[:, half, :], banks[half][:], ACT.Identity, bias=col(c + CONV_B),
                                   scale=col(c + (CONV_B - 1))).then_inc(rg_first, 1)
                for half in range(2):
                    m = i * 2 + half
                    act.wait_ge(rg_gates, m + 3)
                    act.activation(gate_r[:, half, :], banks[4 + half * 2][:], ACT.Sigmoid,
                                   bias=col(m + COLS["rg_ba"]))
                    act.activation(gate_i[:, half, :], banks[5 + half * 2][:], ACT.Sigmoid,
                                   bias=col(m + COLS["rg_bi"]))
                    act.drain()
                    act.sem_inc(rg_sig, 1)
                for half in range(2):
                    at = bass.ds(i * 2 + half, 1) if not isinstance(i, int) else slice(half, half + 1)
                    act.activation(decay[:, half, :], gate_r[:, half, :], ACT.Exp, scale=lam4[:, 0, at])
                    act.activation(half_t[:, half, :], gate_r[:, half, :], ACT.Tanh, scale=lam4[:, 5, at])
                act.drain()
                for half in range(2):
                    act.activation(half_t[:, half, :], half_t[:, half, :], ACT.Sqrt).then_inc(rg_sqrt, 1)
                for half in range(2):
                    act.wait_ge(unit_used, rg.done(i, 2 + half))
                    act.activation(gelu_g[:, half, :], banks[2 + half][:], ACT.Gelu_apprx_tanh).then_inc(rg_gelu, 1)
                    act.drain()
                    act.sem_inc(rg_g_read, 1)
                for half in range(2):
                    act.wait_ge(rg_y, i * 2 + (half + 1))
                    act.copy(one(mix_hi, i * 2 + half), state[:, half, :]).then_inc(mix_hi_ready, 1)

            rg_blocks(0, False)
            with act.Fori(1, rg.iters) as i:
                rg_blocks(i, True)
            rest_of_layer(1)


def _tiles(w):
    k, n = w.shape[0] // P, w.shape[1] // P
    return w.reshape(k, P, n, P).transpose(2, 1, 0, 3).reshape(n, P, k * P)


def _per_channel(v):
    return v.reshape(-1, P).T


def kernel(**inputs):
    import numpy as np
    import concourse.bacc as bacc
    from concourse.bass_utils import run_bass_kernel_spmd

    g = {k: np.asarray(v) for k, v in inputs.items()}
    w_in = g["a_w_in"][0]
    q, k, v = (_tiles(w_in[:, n * D_MODEL:(n + 1) * D_MODEL]) for n in range(3))
    square = [t for j in range(PAIRS) for t in (q[j], k[j], v[j])] + list(_tiles(g["a_w_out"][0]))

    def rest(layer):
        up = _tiles(g["f_w_up"][layer])
        out = [up[half * FT + j] for j in range(FT) for half in range(2)]
        ple = _tiles(g["ple_w"][layer])
        out += [np.concatenate([ple[4 * n + c] for c in range(4)], axis=1) for n in range(2)]
        return out + list(_tiles(g["ple_gate_w"][layer]))

    square += rest(0)
    rg = _tiles(g["b_w_in"][0])
    square += [rg[part * KT + 2 * i + half] for i in range(KT // 2) for part in range(2) for half in range(2)]
    square += list(_tiles(g["b_w_out"][0])) + rest(1)
    columns = []
    for layer in range(DEPTH):
        for name in ("ln1_g", "ln1_b", "ln2_g", "ln2_b", "ple_gate_b"):
            columns.append(_per_channel(g[name][layer]))
        taps = np.stack([*g["f_conv_w"][layer], g["f_conv_b"][layer]])
        taps = taps.reshape(CONV_F + 1, 2, FT, P).transpose(3, 2, 1, 0)
        columns.append(taps.reshape(P, -1))
    taps = np.stack([*g["b_conv_w"][0], g["b_conv_b"][0]]).reshape(CONV_B + 1, KT, P)
    columns.append(taps.transpose(2, 1, 0).reshape(P, -1))
    columns += [_per_channel(g[n][0].reshape(-1)) for n in ("b_b_a", "b_b_i", "b_lam")]

    arrays = {
        "xT": g["x"][0].T.reshape(KT, P, SEQ).transpose(1, 0, 2),
        "pT": g["p"][:, 0].transpose(0, 2, 1).reshape(DEPTH, 2, P, SEQ).transpose(0, 2, 1, 3),
        "w_square": np.stack(square),
        "w_down": np.concatenate([_tiles(g["f_w_down"][layer]) for layer in range(DEPTH)]),
        "w_forget": w_in[:, 3 * D_MODEL:].reshape(KT, P, HEADS).transpose(1, 0, 2),
        "b_forget": g["a_b_f"].reshape(HEADS, 1),
        "w_lru": np.concatenate([g["b_w_a"][0], g["b_w_i"][0]], axis=2),
        "columns": np.concatenate(columns, axis=1),
    }
    arrays = {n: np.ascontiguousarray(a) for n, a in arrays.items()}
    assert arrays["columns"].shape == (P, N_COLS)
    nc = bacc.Bacc("TRN2", target_bir_lowering=False, num_devices=1)
    ins = [nc.dram_tensor(n, a.shape, F32, kind="ExternalInput").ap() for n, a in arrays.items()]
    out = nc.dram_tensor("outT", (KT, P, SEQ), F32, kind="ExternalOutput").ap()
    hybrid_trunk_kernel(nc, *ins, out)
    r = run_bass_kernel_spmd(nc, [arrays], core_ids=[0])
    return np.ascontiguousarray(np.asarray(r.results[0]["outT"]).reshape(D_MODEL, SEQ).T)[None]
```

```python
from contextlib import ExitStack

import concourse.bass as bass
from concourse import mybir

F32 = mybir.dt.float32
F32R = mybir.dt.float32r
BF16 = mybir.dt.bfloat16
ALU = mybir.AluOpType
ACT = mybir.ActivationFunctionType
AX_X = mybir.AxisListType.X

P = 128
SEQ = 512
D_MODEL = 1024
DEPTH = 2
HEADS = 16
HEAD_DIM = D_MODEL // HEADS
D_FF = 2816
D_PLE = 256
CONV_F = 3
CONV_B = 4
LN_EPS = 1e-5
ALPHA = (2.0 * DEPTH) ** 0.25
KT = D_MODEL // P
FT = D_FF // P
PAIRS = HEADS // 2
PLE_TILES = D_PLE // P
QT = SEQ // P
UNIT = KT * P
OUT_TOGETHER = 5
SHIFT_TILES = 3
SLOTS = 4
TURN_AT = 2
FIRST_AT = (1, 1, 4, 5, 6)
SECOND_AT = (0, 1, 3, 4, 5)
GATES_AT = (1, 4)
PARTS_AT = 4
PLE_AT = (1, 3)
EMB_READ = (0, 3, 5, 6, 7, 8, 8, 8, 8, 8)
MASKED = -3.0e38
LOG1P_TERMS = [1.0 / (2 * n + 1) for n in range(9)]

COLS = {}


def _columns():
    at = 0
    for layer in range(DEPTH):
        for name, n in (("ln1_g", KT), ("ln1_b", KT), ("ln2_g", KT), ("ln2_b", KT), ("gate_b", KT),
                        ("conv", 2 * FT * (CONV_F + 1))):
            COLS[name, layer] = at
            at += n
    for name, n in (("rg_conv", KT * (CONV_B + 1)), ("rg_ba", KT), ("rg_bi", KT), ("rg_lam", KT)):
        COLS[name] = at
        at += n
    return at


N_COLS = _columns()


class Phase:

    def __init__(self, slots, iters, widths, first, filled, lead):
        self.slots, self.iters, self.widths, self.first, self.filled, self.lead = (
            slots, iters, widths, first, filled, lead)

    def unit(self, i, r):
        return i * len(self.slots) + (self.first + r)

    def fills(self, i, r):
        s = self.slots[r]
        return i * self.slots.count(s) + (self.filled[s] + self.slots[:r + 1].count(s))

    def slot_free(self, i, r):
        return i * len(self.slots) + (self.first + r + 1 + SLOTS - self.lead[r])

    def done(self, i, r):
        return i * len(self.slots) + (self.first + r + 1 + SLOTS)


def plan():
    whole = [UNIT]
    down = [8 * P, 7 * P, 7 * P]
    want = [("qkv", [0, 1, 2], PAIRS, whole), ("out0", [0, 1, 2, 3], 2, whole),
            ("up0", [0, 1, 2, 3], 2 * FT // 4, whole), ("down0", [0, 1, 2] * 2, KT // 2, down),
            ("ple0", [0, 1], 1, whole), ("gate0", [2, 3, 0, 1], 2, whole),
            ("rg", [2, 3, 0, 1], 2 * KT // 4, whole), ("out1", [2, 3, 0, 1], 2, whole),
            ("up1", [2, 3, 0, 1], 2 * FT // 4, whole), ("down1", [2, 3, 0] * 2, KT // 2, down),
            ("ple1", [2, 3], 1, whole), ("gate1", [0, 1, 2, 3], 2, whole)]
    phases, first, last, filled = {}, 0, [-SLOTS] * SLOTS, [0] * SLOTS
    for name, slots, iters, widths in want:
        lead = [SLOTS] * len(slots)
        before, at = list(filled), first
        for _ in range(iters):
            for r, s in enumerate(slots):
                lead[r] = min(lead[r], at - last[s])
                last[s] = at
                filled[s] += 1
                at += 1
        phases[name] = Phase(slots, iters, (widths * len(slots))[:len(slots)], first, before, lead)
        first = at
    return phases


def hybrid_trunk_kernel(nc, xT, pT, w_square, w_down, w_forget, b_forget, w_lru, columns, outT):
    phases = plan()
    with ExitStack() as ctx:
        def sem(name):
            return ctx.enter_context(nc.semaphore(name))

        start = (nc.sbuf_base + 63) // 64 * 64
        size = 207 * 1024
        ctx.enter_context(nc.sbuf_tensor("arena", [P, size // 4], F32))
        at = [start]

        def place(name, shape, dt, where=None):
            n = 4 if dt != BF16 else 2
            for k in shape[1:]:
                n *= k
            n = (n + 63) // 64 * 64
            where = at if where is None else where
            t = nc.alloc_sbuf_tensor_at(name, shape, dt, offset=where[0])
            where[0] += n
            assert where[0] <= start + size, name
            return t

        x = place("x", [P, KT, SEQ], F32)
        x_hi_at = at[0]
        x_hi = place("x_hi", [P, KT, SEQ], F32R)
        x_lo = place("x_lo", [P, KT, SEQ], F32R)
        stage = place("stage", [P, SLOTS, UNIT], F32)
        w_hi = place("w_hi", [P, SLOTS, UNIT], F32R)
        w_lo = place("w_lo", [P, SLOTS, UNIT], F32R)
        cols = place("cols", [P, N_COLS], F32)
        mean_of = place("mean_of", [P, P], F32)
        ident = place("ident", [P, P], F32)
        ident_bf = place("ident_bf", [P, P], BF16)
        mask_bf = place("mask_bf", [P, P], BF16)
        waiter = place("waiter", [P, 1], F32)
        lam4 = place("lam4", [P, 6, KT], F32)
        less_shift = place("less_shift", [P, 1], F32)
        norm_stat = place("norm_stat", [P, 2 * QT], F32)
        shift_of = place("shift_of", [P, P], F32)
        part_total = place("part_total", [P, SEQ], F32)
        squares = part_total
        shift = place("shift", [P, SEQ], F32)
        dist = place("dist", [P, 2, SEQ], F32)
        total = place("total", [P, SEQ], F32)
        tmp_at = at[0]
        tmp = place("tmp", [P, 4, SEQ], F32)
        p_in = place("p_in", [P, PLE_TILES, SEQ], F32, [x_hi_at])
        a = [tmp_at]
        p_hi = place("p_hi", [P, PLE_TILES, SEQ], F32R, a)
        p_lo = place("p_lo", [P, PLE_TILES, SEQ], F32R, a)
        shared = at[0]
        a = [shared]
        h_hi = place("h_hi", [P, FT, SEQ], F32R, a)
        h_lo = place("h_lo", [P, FT, SEQ], F32R, a)
        a = [shared]
        mix_hi = place("mix_hi", [P, KT, SEQ], F32R, a)
        mix_lo = place("mix_lo", [P, KT, SEQ], F32R, a)
        b = list(a)
        q_a = place("q_a", [P, 2, SEQ], F32R, a)
        k_a = place("k_a", [P, 2, SEQ], F32R, a)
        q_b = place("q_b", [P, 2, SEQ], F32R, a)
        k_b = place("k_b", [P, 2, SEQ], F32R, a)
        v_chan = place("v_chan", [P, SEQ], F32, a)
        v_tok = place("v_tok", [P, QT, P], F32, a)
        tri = QT * (QT + 1) // 2 * P
        probs = place("probs", [P, 2, tri], F32, a)
        probs_t = place("probs_t", [P, tri], F32, a)
        z_chan = place("z_chan", [HEADS, SEQ], F32, a)
        fg = place("fg", [P, 6, QT * HEADS], F32, a)
        up_to = place("up_to", [P, SEQ], F32, a)
        c_rows = place("c_rows", [HEADS, 2, SEQ], F32R, a)
        wf = place("wf", [P, KT, HEADS], F32, a)
        bf = place("bf", [HEADS, 1], F32, a)
        stat = place("stat", [P, 2, 12], F32, a)
        a = list(b)
        w_ai = place("w_ai", [P, 2, 2 * P], F32, a)
        conv_x = place("conv_x", [P, 2, SEQ], F32, a)
        half_t = place("half_t", [P, 2, SEQ], F32, a)
        decay = place("decay", [P, 2, SEQ], F32, a)
        drive = place("drive", [P, SEQ], F32, a)
        state = place("state", [P, 2, SEQ], F32, a)
        gelu_g = place("gelu_g", [P, 2, SEQ], F32, a)
        g = [tmp_at]
        gate_r = place("gate_r", [P, 2, SEQ], F32, g)
        gate_i = place("gate_i", [P, 2, SEQ], F32, g)
        next_at = shared + 2 * FT * SEQ * 4 - 2 * KT * SEQ * 4
        assert a[0] <= next_at
        a = [b[0] + 4 * 4 * P]
        emb = place("emb", [P, KT, SEQ], F32, a)
        assert a[0] <= next_at
        a = [next_at]
        next_hi = place("next_hi", [P, KT, SEQ], F32R, a)
        next_lo = place("next_lo", [P, KT, SEQ], F32R, a)

        banks = [ctx.enter_context(nc.psum_tensor(f"bank{n}", [P, SEQ], F32)) for n in range(8)]
        c_dram = nc.dram_tensor("forget_rows", (HEADS, 2, SEQ), F32, kind="Internal").ap()

        unit_loaded = [sem(f"unit_loaded{s}") for s in range(SLOTS)]
        unit_split = sem("unit_split")
        unit_used = sem("unit_used")
        x_loaded = [sem(f"x_loaded{n}") for n in range(KT // 2)]
        fg_w_loaded, cols_loaded = sem("fg_w_loaded"), sem("cols_loaded")
        consts_set = sem("consts_set")
        x_hi_ready, x_lo_ready = sem("x_hi_ready"), sem("x_lo_ready")
        mix_hi_ready, mix_lo_ready = sem("mix_hi_ready"), sem("mix_lo_ready")
        fg_done, fg_chan, fg_turned, fg_abs, fg_exp, fg_steps, fg_summed, fg_rows = (
            sem(n) for n in ("fg_done", "fg_chan", "fg_turned", "fg_abs", "fg_exp", "fg_steps", "fg_summed",
                             "fg_rows"))
        fg_stored, row_loaded = sem("fg_stored"), sem("row_loaded")
        q_read, q_ready, kv_read, k_ready = sem("q_read"), sem("q_ready"), sem("kv_read"), sem("k_ready")
        vt_done, vt_read = sem("vt_done"), sem("vt_read")
        s_done, max_ready, exp_ready, probs_ready = (sem("s_done"), sem("max_ready"), sem("exp_ready"),
                                                     sem("probs_ready"))
        pt_done, pt_read, pv_done = sem("pt_done"), sem("pt_read"), sem("pv_done")
        o_read = sem("o_read")
        tile_read = {n: sem(f"{n}_read") for n in phases if n not in ("qkv", "rg")}
        part_sum, shift_done, shift_ready, parts_ready, sum_ready, mean_done, var_done, var_ready = (
            sem(n) for n in ("part_sum", "shift_done", "shift_ready", "parts_ready", "sum_ready", "mean_done",
                             "var_done", "var_ready"))
        dev_ready, diag_ready, spread_done, scaled = (
            sem(n) for n in ("dev_ready", "diag_ready", "spread_done", "scaled"))
        dist_ready, square_done = sem("dist_ready"), sem("square_done")
        conv_first, conv_done, gelu_done, h_ready, h_hi_ready, h_lo_ready = (
            sem(n) for n in ("conv_first", "conv_done", "gelu_done", "h_ready", "h_hi_ready", "h_lo_ready"))
        p_loaded, p_hi_ready, p_lo_ready, gated, emb_added = (
            sem(n) for n in ("p_loaded", "p_hi_ready", "p_lo_ready", "gated", "emb_added"))
        lru_w_loaded = [sem(f"lru_w_loaded{n}") for n in range(2)]
        lam_exp, lam_abs = sem("lam_exp"), sem("lam_abs")
        rg_first, rg_conv, rg_gates, rg_sig, rg_sqrt, rg_gelu, rg_y = (
            sem(n) for n in ("rg_first", "rg_conv", "rg_gates", "rg_sig", "rg_sqrt", "rg_gelu", "rg_y"))
        rg_x_read, rg_g_read, emb_done = sem("rg_x_read"), sem("rg_g_read"), sem("emb_done")
        stored = sem("stored")

        block = ctx.enter_context(nc.Block())

        def unit_start(widths, r):
            return sum(widths[:r % 3])

        def one(t, m):
            return t[:, m, :] if isinstance(m, int) else t[:, bass.ds(m, 1), :].rearrange("p a n -> p (a n)")

        def next_tiles(r):
            return ((), (0,), (1,), (2, 3))[r]

        @block.sync
        def _(sp):
            for n in range(KT // 4):
                sp.dma_start(x[:, 2 * n:2 * n + 2, :], xT[:, 2 * n:2 * n + 2, :]).then_inc(x_loaded[n], 16)
            square_first = [0]
            for name, ph in phases.items():
                base = square_first[0]
                n = len(ph.slots)
                with sp.Fori(0, ph.iters) as i:
                    for r, s in enumerate(ph.slots):
                        sp.wait_ge(unit_split, ph.slot_free(i, r))
                        w = ph.widths[r]
                        if name.startswith("down"):
                            c = unit_start(ph.widths, r)
                            src = w_down[bass.ds(i * (n // 3) + (int(name[-1]) * KT + r // 3), 1), :, c:c + w]
                        else:
                            src = w_square[bass.ds(i * n + (base + r), 1), :, :]
                        sp.dma_start(stage[:, s, 0:w],
                                     src.rearrange("a p n -> (a p) n")).then_inc(unit_loaded[s], 16)
                    if name == "rg":
                        for half in range(2):
                            sp.wait_ge(rg_gates, i * 2 + (half + 1))
                            sp.dma_start(w_ai[:, half, :], w_lru[bass.ds(i * 2 + half, 1), :, :]
                                         .rearrange("a p n -> (a p) n")).then_inc(lru_w_loaded[half], 16)
                if not name.startswith("down"):
                    square_first[0] += ph.iters * n
            for m in range(KT):
                sp.wait_ge(emb_added, 4 + KT + m + 1)
                sp.dma_start(outT[m], x[:, m, :]).then_inc(stored, 16)
            sp.wait_ge(stored, 16 * KT)

        @block.gpsimd
        def _(pool):
            pool.sem_inc(unit_split, SLOTS)
            pool.memset(waiter[:], 0.0)
            pool.memset(shift_of[:], 1.0 / (SHIFT_TILES * P))
            pool.memset(mean_of[:], 1.0 / D_MODEL)
            pool.memset(less_shift[:], -1.0 / P)
            pool.memset(ident[:], 1.0)
            pool.memset(ident_bf[:], 1.0)
            pool.memset(mask_bf[:], 0.0)
            pool.memset(up_to[:], 1.0)
            pool.drain()
            pool.memset(q_a[HEAD_DIM:HEAD_DIM + 2, :, :].bitcast(F32), 1.0)
            pool.drain()
            for m in (ident, ident_bf):
                pool.affine_select(out=m[:], in_=m[:], compare_op=ALU.is_equal, fill=0.0, base=0,
                                   pattern=[[-1, P]], channel_multiplier=1)
            pool.affine_select(out=up_to[:, 0:P], in_=up_to[:, 0:P], compare_op=ALU.is_ge, fill=0.0, base=0,
                               pattern=[[1, P]], channel_multiplier=-1)
            pool.affine_select(out=mask_bf[:], in_=mask_bf[:], compare_op=ALU.is_ge, fill=MASKED, base=0,
                               pattern=[[-1, P]], channel_multiplier=1)
            pool.drain()
            pool.sem_inc(consts_set, 1)
            for ph in phases.values():
                with pool.Fori(0, ph.iters) as i:
                    for r, s in enumerate(ph.slots):
                        w = ph.widths[r]
                        pool.wait_ge(unit_loaded[s], ph.fills(i, r) * 16)
                        pool.wait_ge(unit_used, ph.slot_free(i, r))
                        pool.tensor_tensor(waiter[:], waiter[:], waiter[:], ALU.mult)
                        pool.drain()
                        pool.tensor_scalar(w_hi[:, s, 0:w], stage[:, s, 0:w], 1.0, 0.0, ALU.mult, ALU.add)
                        pool.drain()
                        pool.tensor_tensor(w_lo[:, s, 0:w], stage[:, s, 0:w], w_hi[:, s, 0:w].bitcast(F32),
                                           ALU.subtract).then_inc(unit_split, 1)

        @block.tensor
        def _(pe):
            pe.sem_inc(unit_used, SLOTS)

            def unit_ready(ph, i, r):
                pe.wait_ge(unit_split, ph.done(i, r))

            def three(out, s, c, m_hi, m_lo, first, last):
                pe.matmul(out, w_hi[:, s, c:c + P], m_hi, start=first, stop=False)
                pe.matmul(out, w_hi[:, s, c:c + P], m_lo, start=False, stop=False)
                return pe.matmul(out, w_lo[:, s, c:c + P], m_hi, start=False, stop=last)

            def whole_tile(ph, i, r, bank, hi, lo, beside={}):
                unit_ready(ph, i, r)
                for k in range(KT):
                    if k - 1 in beside:
                        beside[k - 1]()
                    mm = three(banks[bank][:], ph.slots[r], k * P, hi[:, k, :], lo[:, k, :], k == 0, k == KT - 1)
                mm.then_inc(unit_used, 1)

            def norm_shift(n):
                pe.wait_ge(part_sum, n + 1)
                pe.matmul(banks[6][:], shift_of[:], part_total[:], start=True, stop=True).then_inc(shift_done, 1)

            def token_sums(c, src, weights, start, stop):
                for t in range(QT):
                    mm = pe.matmul(banks[6][:, c + t:c + t + 1], src[:, t * P:(t + 1) * P], weights,
                                   start=start and t == 0, stop=stop, skip_group_check=True)
                return mm

            def norm_parts(n, step):
                if step == 0:
                    pe.wait_ge(parts_ready, n + 1)
                    pe.matmul(banks[7][:], mean_of[:], total[:], start=True, stop=False)
                    token_sums(0, shift, less_shift[:], True, False)
                if step == 1:
                    token_sums(0, total, mean_of[:, 0:1], False, False)
                if step == 2:
                    token_sums(QT, squares, mean_of[:, 0:1], False, False)

            def norm_sums(n):
                pe.wait_ge(sum_ready, n + 1)
                pe.matmul(banks[7][:], mean_of[:], x[:, KT - 1, :], start=False, stop=True).then_inc(mean_done, 1)
                token_sums(0, x[:, KT - 1, :], mean_of[:, 0:1], False, True)
                pe.wait_ge(square_done, (n + 1) * KT)
                token_sums(QT, dist[:, (KT - 1) % 2, :], mean_of[:, 0:1], False, True).then_inc(var_done, 1)

            def norm_spread(n):
                for t in range(QT):
                    pe.wait_ge(diag_ready, n * QT + t + 1)
                    mm = pe.matmul(banks[6][:, t * P:(t + 1) * P], mean_of[:], dist[:, 0, t * P:(t + 1) * P],
                                   start=True, stop=True, skip_group_check=True)
                mm.then_inc(spread_done, 1)

            pe.wait_ge(fg_w_loaded, 32)
            for k in range(KT):
                if k % 2 == 0:
                    pe.wait_ge(x_loaded[k // 2], 16)
                mm = pe.matmul(banks[5][0:HEADS, :], wf[:, k, :], x[:, k, :], start=(k == 0), stop=(k == KT - 1))
            mm.then_inc(fg_done, 1)

            def turn_forget():
                pe.wait_ge(consts_set, 1)
                pe.wait_ge(fg_chan, 1)
                for t in range(QT):
                    mm = pe.transpose(banks[6][:, t * HEADS:(t + 1) * HEADS], z_chan[:, t * P:(t + 1) * P],
                                      ident[0:HEADS, 0:HEADS])
                mm.then_inc(fg_turned, 1)

            def sum_forget():
                pe.wait_ge(fg_steps, 1)
                for t in range(QT):
                    mm = pe.matmul(banks[7][0:HEADS, t * P:SEQ], fg[:, 5, t * HEADS:(t + 1) * HEADS],
                                   up_to[:, 0:SEQ - t * P], start=(t == 0), stop=(t == QT - 1),
                                   skip_group_check=True)
                mm.then_inc(fg_summed, 1)

            qkv = phases["qkv"]
            S_AT = [(3, 384), (4, 0), (3, 0), (2, 0)]

            def project(j, r, bank, beside={}):
                whole_tile(qkv, j, r, bank, x_hi, x_lo, beside)

            def scores(j, h):
                pe.wait_ge(exp_ready, j * 8 + (h * 4 + 1))
                if h == 0:
                    pe.wait_ge(q_ready, j + 1)
                    pe.wait_ge(k_ready, j + 1)
                    pe.wait_ge(row_loaded, j * 16 + 16)
                for t in (3, 2, 0, 1):
                    bank, c = S_AT[t]
                    w = (t + 1) * P
                    pe.matmul(banks[bank][:, c:c + w], q_a[0:HEAD_DIM + 2, h, t * P:(t + 1) * P],
                              k_a[0:HEAD_DIM + 2, h, 0:w], start=True, stop=False, skip_group_check=True)
                    pe.matmul(banks[bank][:, c:c + w], q_b[:, h, t * P:(t + 1) * P], k_b[:, h, 0:w],
                              start=False, stop=False, skip_group_check=True)
                    mm = pe.matmul(banks[bank][:, c + w - P:c + w], ident_bf[:], mask_bf[:], start=False,
                                   stop=True, skip_group_check=True)
                mm.then_inc(s_done, 1)

            PT_AT = [(5, 0), (6, 0), (5, 0), (5, 256)]

            def turn_probs(j, h, step):
                if step == 0:
                    pe.wait_ge(probs_ready, j * 2 + (h + 1))
                pe.wait_ge(pt_read, j * 6 + (h * 3 + max(step, 1)))
                for kt in ((0,), (1,), (2, 3))[step]:
                    bank, c = PT_AT[kt]
                    for t in range(kt, QT):
                        a0 = (t * (t + 1) // 2 + kt) * P
                        mm = pe.transpose(banks[bank][:, c + (t - kt) * P:c + (t - kt + 1) * P],
                                          probs[:, h, a0:a0 + P], ident[:])
                mm.then_inc(pt_done, 1)

            def sum_values(j, h, tiles):
                if h == 0 and tiles[0] == 0:
                    pe.wait_ge(vt_read, j + 1)
                for kt in tiles:
                    w, c0 = (QT - kt) * P, sum(QT - t for t in range(kt)) * P
                    pe.wait_ge(pt_read, j * 6 + (h * 3 + min(kt, 2) + 2))
                    mm = pe.matmul(banks[7][h * HEAD_DIM:(h + 1) * HEAD_DIM, kt * P:SEQ],
                                   v_tok[:, kt, h * HEAD_DIM:(h + 1) * HEAD_DIM], probs_t[:, c0:c0 + w],
                                   start=(kt == 0), stop=(kt == QT - 1), skip_group_check=True)
                if tiles[-1] == QT - 1:
                    mm.then_inc(pv_done, 1)

            def turn_values(j):
                pe.wait_ge(kv_read, j * 2 + 2)
                pe.wait_ge(o_read, j + 1)
                for t in range(QT):
                    mm = pe.transpose(banks[7][:, t * P:(t + 1) * P], v_chan[:, t * P:(t + 1) * P], ident[:])
                mm.then_inc(vt_done, 1)

            def head(j, h, at):
                steps = (lambda: turn_probs(j, h, 0), lambda: turn_probs(j, h, 1),
                         lambda: turn_probs(j, h, 2), lambda: sum_values(j, h, (0, 1)),
                         lambda: sum_values(j, h, (2, 3)))
                beside = {}
                for k, step in zip(at, steps):
                    beside.setdefault(k, []).append(step)
                return {k: (lambda todo=todo: [step() for step in todo]) for k, todo in beside.items()}

            pe.wait_ge(x_lo_ready, KT)
            project(0, 0, 0, {1: turn_forget})
            project(0, 1, 1, {3: sum_forget})
            pe.wait_ge(q_read, 1)
            project(0, 2, 0)
            with pe.Fori(1, PAIRS) as j:
                scores(j - 1, 0)
                pe.wait_ge(kv_read, j * 2)
                project(j, 0, 0, {TURN_AT: lambda: turn_values(j - 1)})
                scores(j - 1, 1)
                project(j, 1, 1, head(j - 1, 0, FIRST_AT))
                pe.wait_ge(q_read, j + 1)
                project(j, 2, 0, head(j - 1, 1, SECOND_AT))
            EARLY_OUT = [(k, r) for r in range(3) for k in range(KT - 1)]

            def early_out(r, beside):
                unit_ready(phases["out0"], 0, r)
                for k, _ in EARLY_OUT[:KT - 1]:
                    if r == 0:
                        pe.wait_ge(mix_lo_ready, k + 1)
                    three(banks[r][:], phases["out0"].slots[r], k * P, mix_hi[:, k, :], mix_lo[:, k, :],
                          k == 0, False)
                    if k in beside:
                        beside[k]()

            scores(PAIRS - 1, 0)
            pe.wait_ge(kv_read, PAIRS * 2)
            early_out(0, {TURN_AT: lambda: turn_values(PAIRS - 1)})
            scores(PAIRS - 1, 1)
            early_out(1, head(PAIRS - 1, 0, FIRST_AT))
            pe.wait_ge(exp_ready, PAIRS * 8 + 1)
            early_out(2, head(PAIRS - 1, 1, SECOND_AT))

            def square_phase(name, hi, lo, hi_ready, lo_ready, count, together, wide, between=None,
                             bank_free=None, started=(), beside_last={}):
                ph = phases[name]
                high, low = "high", "low"
                steps = [(k, r, part) for k in range(together) for part in (high, low) for r in range(wide)]
                steps += [(k, r, part) for r in range(wide, 4) for k in range(together) for part in (high, low)]
                steps += [(k, r, part) for r in range(4) for k in range(together, KT) for part in (high, low)]
                waited = set()
                for k, r, part in steps:
                    if (k, r) in started:
                        continue
                    if k == 0 and part == high:
                        unit_ready(ph, 0, r)
                        pe.wait_ge(tile_read[name], r + 1)
                        if bank_free is not None:
                            bank_free(r)
                    if (k, part) not in waited:
                        waited.add((k, part))
                        pe.wait_ge(hi_ready if part == high else lo_ready, count + k + 1)
                    s, c = ph.slots[r], k * P
                    if part == high:
                        pe.matmul(banks[r][:], w_hi[:, s, c:c + P], hi[:, k, :], start=(k == 0), stop=False)
                        pe.matmul(banks[r][:], w_lo[:, s, c:c + P], hi[:, k, :], start=False, stop=False)
                    else:
                        mm = pe.matmul(banks[r][:], w_hi[:, s, c:c + P], lo[:, k, :], start=False, stop=(k == KT - 1))
                        if k == KT - 1:
                            mm.then_inc(unit_used, 1)
                if between is not None:
                    between()
                with pe.Fori(1, ph.iters) as i:
                    for r in range(4):
                        pe.wait_ge(tile_read[name], i * 4 + (r + 1))
                        whole_tile(ph, i, r, r, hi, lo, beside_last if r == 3 else {})

            def down_tile(name, layer, i, half, beside={}):
                ph = phases[name]
                pe.wait_ge(tile_read[name], i * 2 + (half + 1))
                k = 0
                for part in range(3):
                    r = half * 3 + part
                    unit_ready(ph, i, r)
                    for c in range(ph.widths[r] // P):
                        if k >= FT - 4:
                            pe.wait_ge(h_lo_ready, layer * FT + 2 + k + 1)
                        if k - 1 in beside:
                            beside[k - 1]()
                        mm = three(banks[half][:], ph.slots[r], c * P, h_hi[:, k, :], h_lo[:, k, :],
                                   k == 0, k == FT - 1)
                        k += 1
                    mm.then_inc(unit_used, 1)

            def down_rounds(name, layer, a, b):
                with pe.Fori(a, b) as i:
                    for half in range(2):
                        down_tile(name, layer, i, half)

            def ple_tiles(name, layer, a, b):
                ph = phases[name]
                for m in range(a, b):
                    r, c = m // 4, m % 4
                    if c == 0:
                        unit_ready(ph, 0, r)
                    pe.wait_ge(p_lo_ready, (layer + 1) * 2)
                    if m >= 4:
                        pe.wait_ge(tile_read[name], m - 3)
                    for k in range(PLE_TILES):
                        mm = three(banks[2 + m % 4][:], ph.slots[r], (c * 2 + k) * P, p_hi[:, k, :], p_lo[:, k, :],
                                   k == 0, k == 1)
                    mm.then_inc(emb_done, 1)
                    if c == 3:
                        pe.wait_ge(emb_done, layer * KT + m + 1)
                        pe.sem_inc(unit_used, 1)
                if b == KT:
                    pe.wait_ge(tile_read[name], KT - 2)

            def rest_of_layer(layer):
                square_phase(f"out{layer}", mix_hi, mix_lo, mix_hi_ready, mix_lo_ready, layer * KT,
                             OUT_TOGETHER, 4, lambda: norm_shift(2 * layer),
                             rg_bank_free if layer else None, () if layer else EARLY_OUT,
                             {PARTS_AT + step: (lambda step=step: norm_parts(2 * layer, step)) for step in range(3)})
                norm_sums(2 * layer)
                norm_spread(2 * layer)
                square_phase(f"up{layer}", x_hi, x_lo, x_hi_ready, x_lo_ready, (layer * 3 + 1) * KT, KT, 3)
                pe.wait_ge(tile_read[f"up{layer}"], 4 + 2 * FT - 2)
                down_rounds(f"down{layer}", layer, 0, KT // 4)
                norm_shift(2 * layer + 1)
                down_rounds(f"down{layer}", layer, KT // 4, KT // 2 - 1)
                down_tile(f"down{layer}", layer, KT // 2 - 1, 0)
                down_tile(f"down{layer}", layer, KT // 2 - 1, 1, 
                          {2 * KT - 4 + 2 * step: (lambda step=step: norm_parts(2 * layer + 1, step))
                           for step in range(3)})
                ple_tiles(f"ple{layer}", layer, 0, PLE_AT[0])
                norm_sums(2 * layer + 1)
                ple_tiles(f"ple{layer}", layer, PLE_AT[0], PLE_AT[1])
                norm_spread(2 * layer + 1)
                ple_tiles(f"ple{layer}", layer, PLE_AT[1], KT)
                square_phase(f"gate{layer}", x_hi, x_lo, x_hi_ready, x_lo_ready, (layer * 3 + 2) * KT, KT, 3)

            def rg_bank_free(r):
                pe.wait_ge((rg_x_read, rg_g_read)[r // 2], KT + 1 + r % 2)

            rest_of_layer(0)

            rg = phases["rg"]
            pe.sem_inc(rg_gates, 2)

            def rg_gate_products(i, half):
                pe.wait_ge(rg_conv, i * 2 + (half + 1))
                pe.wait_ge(lru_w_loaded[half], (i + 1) * 16)
                pe.wait_ge(rg_sig, i * 2 + (half + 1))
                pe.matmul(banks[4 + half * 2][:], w_ai[:, half, 0:P], conv_x[:, half, :], start=True, stop=True)
                pe.matmul(banks[5 + half * 2][:], w_ai[:, half, P:2 * P], conv_x[:, half, :], start=True,
                          stop=True).then_inc(rg_gates, 1)

            def rg_round(i, first):
                for r in range(4):
                    if first:
                        pe.wait_ge(tile_read["gate0"], 4 + KT - 3 + r)
                    if r == 0 and first:
                        pe.wait_ge(x_lo_ready, 3 * KT + 1)
                    pe.wait_ge((rg_x_read, rg_g_read)[r // 2], i * 2 + (r % 2 + 1))
                    beside = {}
                    if first and r == 0:
                        beside = {k: (lambda k=k: pe.wait_ge(x_lo_ready, 3 * KT + k + 2)) for k in range(KT - 1)}
                    if r == 2:
                        beside = {GATES_AT[half]: (lambda half=half: rg_gate_products(i, half)) for half in range(2)}
                    whole_tile(rg, i, r, r, next_hi, next_lo, beside)

            rg_round(0, True)
            with pe.Fori(1, rg.iters) as i:
                rg_round(i, False)
            rest_of_layer(1)

        @block.vector
        def _(dve):
            def log1p_twice(q, e, den, q2, acc):
                dve.tensor_scalar(den, e, 2.0, None, ALU.add)
                dve.drain()
                dve.reciprocal(q2, den)
                dve.drain()
                dve.tensor_tensor(q, e, q2, ALU.mult)
                dve.drain()
                dve.tensor_tensor(q2, q, q, ALU.mult)
                dve.drain()
                dve.tensor_scalar(acc, q2, LOG1P_TERMS[-1], None, ALU.mult)
                dve.drain()
                for c in LOG1P_TERMS[-2:0:-1]:
                    dve.scalar_tensor_tensor(acc, acc, c, q2, ALU.add, ALU.mult)
                    dve.drain()
                dve.scalar_tensor_tensor(acc, acc, LOG1P_TERMS[0], q, ALU.add, ALU.mult)
                dve.drain()

            def norm_tile(n, m):
                xm = x[:, m, :]
                dve.tensor_tensor(dist[:, m % 2, :], xm, shift[:], ALU.subtract).then_inc(dist_ready, 1)

            def layer_norm(n, layer, g):
                def center(m):
                    dve.tensor_tensor(x[:, m, :], x[:, m, :], banks[7][:], ALU.subtract)

                dve.wait_ge(mean_done, n + 1)
                center(0)
                center(1)
                dve.wait_ge(var_done, n + 1)
                dve.tensor_copy(norm_stat[:, 0:QT], banks[6][:, 0:QT])
                dve.drain()
                dve.tensor_tensor(norm_stat[:, 0:QT], banks[6][:, 0:QT], norm_stat[:, 0:QT], ALU.mult)
                dve.drain()
                dve.tensor_tensor(norm_stat[:, QT:2 * QT], banks[6][:, QT:2 * QT], norm_stat[:, 0:QT],
                                  ALU.subtract).then_inc(var_ready, 1)
                dve.wait_ge(dev_ready, n + 1)
                dve.reciprocal(norm_stat[:, 0:QT], norm_stat[:, QT:2 * QT])
                dve.drain()
                for t in range(QT):
                    dve.tensor_scalar(dist[:, 0, t * P:(t + 1) * P], ident[:], norm_stat[:, t:t + 1],
                                      float(D_MODEL), ALU.mult, ALU.mult).then_inc(diag_ready, 1)
                center(2)
                center(3)
                dve.drain()
                dve.wait_ge(spread_done, n + 1)
                for m in range(KT + 1):
                    if m < KT:
                        c = COLS[g, layer] + m
                        dve.scalar_tensor_tensor(x[:, m, :], x[:, m, :], cols[:, c:c + 1], banks[6][:],
                                                 ALU.mult, ALU.mult).then_inc(scaled, 1)
                    if m > 0:
                        dve.wait_ge(x_hi_ready, (x_round[0] * KT) + m)
                        dve.tensor_tensor(x_lo[:, m - 1, :], x[:, m - 1, :], x_hi[:, m - 1, :].bitcast(F32),
                                          ALU.subtract).then_inc(x_lo_ready, 1)
                    if m + 4 < KT:
                        center(m + 4)
                    dve.drain()
                x_round[0] += 1

            x_round = [0]

            def residual_phase(name, n, per_round, units):
                ph = phases[name]

                def residual(i, r, add_from, add_to):
                    dve.wait_ge(unit_used, ph.done(i, (r + 1) * units - 1))
                    xm = x[:, bass.ds(i * per_round + r, 1), :].rearrange("p a n -> p (a n)") \
                        if not isinstance(i, int) else x[:, i * per_round + r, :]
                    dve.scalar_tensor_tensor(xm, xm, ALPHA, banks[r][:], ALU.mult,
                                             ALU.add).then_inc(tile_read[name], 1)
                    dve.drain()
                    if add_from is not None:
                        dve.tensor_tensor(add_to, add_from, xm, ALU.add)

                def add_square(m, first):
                    dve.wait_ge(square_done, n * KT + m + 1)
                    if first:
                        dve.tensor_copy(squares[:], dist[:, 0, :])
                    else:
                        dve.tensor_tensor(squares[:], squares[:], dist[:, m % 2, :], ALU.add)
                    dve.drain()

                tiles = [(m // per_round, m % per_round) for m in range(KT)]
                residual(*tiles[0], None, None)
                residual(*tiles[1], x[:, 0, :], part_total[:])
                residual(*tiles[2], part_total[:], part_total[:])
                dve.drain()
                dve.sem_inc(part_sum, 1)
                residual(*tiles[3], part_total[:], total[:])
                dve.wait_ge(shift_ready, n + 1)
                for m in range(KT):
                    if m == KT - 1:
                        add_square(m - 1, False)
                        dve.sem_inc(parts_ready, 1)
                        residual(*tiles[m], None, None)
                        dve.sem_inc(sum_ready, 1)
                    elif m >= 4:
                        residual(*tiles[m], total[:], total[:])
                    norm_tile(n, m)
                    if 0 < m < KT - 1:
                        add_square(m - 1, m == 1)

            for m in range(KT):
                dve.wait_ge(x_hi_ready, m + 1)
                dve.tensor_tensor(x_lo[:, m, :], x[:, m, :], x_hi[:, m, :].bitcast(F32),
                                  ALU.subtract).then_inc(x_lo_ready, 1)
            x_round[0] = 1

            dve.wait_ge(fg_done, 1)
            dve.tensor_scalar(z_chan[:], banks[5][0:HEADS, :], bf[:, 0:1], None, ALU.add).then_inc(fg_chan, 1)
            z, e, r0, r1, acc, minus_log = (fg[:, n, :] for n in range(6))
            dve.wait_ge(fg_turned, 1)
            dve.tensor_copy(z, banks[6][:, 0:QT * HEADS])
            dve.drain()
            dve.scalar_tensor_tensor(e, z, -1.0, z, ALU.mult, ALU.max).then_inc(fg_abs, 1)
            dve.wait_ge(fg_exp, 1)
            log1p_twice(r0, e, r1, r1, acc)
            dve.tensor_scalar(z, z, -1.0, 0.0, ALU.mult, ALU.max)
            dve.drain()
            dve.scalar_tensor_tensor(minus_log, acc, 2.0, z, ALU.mult, ALU.add).then_inc(fg_steps, 1)

            lz, le, l0, l1, l2 = (lam4[:, n, :] for n in range(5))
            c = COLS["rg_lam"]
            dve.wait_ge(cols_loaded, 16)
            dve.tensor_scalar(lz, cols[:, c:c + KT], -1.0, None, ALU.mult)
            dve.drain()
            dve.tensor_tensor(le, lz, cols[:, c:c + KT], ALU.max).then_inc(lam_abs, 1)

            def queries(j, scored):
                dve.wait_ge(unit_used, phases["qkv"].done(j, 0))
                if scored:
                    dve.wait_ge(s_done, j * 2)
                for h in range(2):
                    dve.tensor_scalar(q_a[0:HEAD_DIM, h, :], banks[0][h * HEAD_DIM:(h + 1) * HEAD_DIM, :],
                                      HEAD_DIM ** -0.5, None, ALU.mult)
                dve.drain()
                for h in range(2):
                    dve.scalar_tensor_tensor(q_b[0:HEAD_DIM, h, :], banks[0][h * HEAD_DIM:(h + 1) * HEAD_DIM, :],
                                             HEAD_DIM ** -0.5, q_a[0:HEAD_DIM, h, :].bitcast(F32), ALU.mult,
                                             ALU.subtract)
                dve.drain()
                dve.sem_inc(q_read, 1)
                dve.tensor_copy(q_b[HEAD_DIM:P, :, :], q_a[0:HEAD_DIM, :, :])
                dve.drain()
                dve.sem_inc(q_ready, 1)

            def keys_low(j):
                dve.wait_ge(kv_read, j * 2 + 1)
                for h in range(2):
                    dve.tensor_tensor(k_b[HEAD_DIM:P, h, :], banks[1][h * HEAD_DIM:(h + 1) * HEAD_DIM, :],
                                      k_a[0:HEAD_DIM, h, :].bitcast(F32), ALU.subtract)
                dve.drain()
                dve.sem_inc(k_ready, 1)

            def maxima(j, h):
                dve.wait_ge(s_done, j * 2 + (h + 1))
                for t, (bank, c) in ((3, (2, 0)), (2, (3, 0)), (0, (3, 384)), (1, (4, 0))):
                    mx = dve.tensor_reduce(stat[:, h, t:t + 1], banks[bank][:, c:c + (t + 1) * P], AX_X, ALU.max,
                                           negate=True)
                    mx.then_inc(max_ready, 1)

            def normalise(j, h):
                dve.wait_ge(exp_ready, j * 8 + (h * 4 + 5))
                dve.reciprocal(stat[:, h, 8:12], stat[:, h, 4:8])
                dve.drain()
                for t in range(QT):
                    a0, w = t * (t + 1) // 2 * P, (t + 1) * P
                    nm = dve.tensor_scalar(probs[:, h, a0:a0 + w], probs[:, h, a0:a0 + w],
                                           stat[:, h, 8 + t:9 + t], None, ALU.mult)
                dve.drain()
                dve.sem_inc(probs_ready, 1)

            def mixed(j):
                dve.wait_ge(mix_hi_ready, j + 1)
                lo = mix_lo[:, bass.ds(j, 1), :].rearrange("p a n -> p (a n)")
                hi = mix_hi[:, bass.ds(j, 1), :].rearrange("p a n -> p (a n)")
                dve.tensor_tensor(lo, banks[7][:], hi.bitcast(F32), ALU.subtract)
                dve.drain()
                dve.sem_inc(mix_lo_ready, 1)
                dve.sem_inc(o_read, 1)

            dve.sem_inc(o_read, 1)
            queries(0, False)
            dve.wait_ge(fg_summed, 1)
            dve.tensor_copy(c_rows[:, 0, :], banks[7][0:HEADS, :])
            dve.drain()
            dve.tensor_tensor(c_rows[:, 1, :], banks[7][0:HEADS, :], c_rows[:, 0, :].bitcast(F32),
                              ALU.subtract).then_inc(fg_rows, 1)
            keys_low(0)
            dve.wait_ge(lam_exp, 1)
            log1p_twice(l0, le, l1, l1, l2)
            dve.tensor_scalar(lz, lz, 0.0, 4.0, ALU.max, ALU.mult)
            dve.drain()
            dve.scalar_tensor_tensor(lam4[:, 5, :], l2, 8.0, lz, ALU.mult, ALU.add)
            dve.drain()
            dve.tensor_scalar(lz, lam4[:, 5, :], -2.0, None, ALU.mult).then_inc(lam_abs, 1)
            with dve.Fori(1, PAIRS) as j:
                maxima(j - 1, 0)
                normalise(j - 1, 0)
                maxima(j - 1, 1)
                normalise(j - 1, 1)
                queries(j, True)
                keys_low(j)
                dve.wait_ge(pv_done, j * 2)
                mixed(j - 1)
            maxima(PAIRS - 1, 0)
            normalise(PAIRS - 1, 0)
            maxima(PAIRS - 1, 1)
            normalise(PAIRS - 1, 1)
            mixed(PAIRS - 1)

            def conv_ffn(layer):
                name = f"up{layer}"
                base = COLS["conv", layer]
                with dve.Fori(0, FT // 2) as i:
                    for half in range(2):
                        for part in (1, 0):
                            r = half * 2 + part
                            c = (i * 4 + r) * (CONV_F + 1) + base
                            t = tmp[:, r, :]
                            dve.wait_ge(conv_first, layer * 2 * FT + i * 4 + (half * 2 + (2 - part)))
                            dve.scalar_tensor_tensor(t[:, 1:SEQ], banks[r][:, 0:SEQ - 1], cols[:, bass.ds(c + 1, 1)],
                                                     t[:, 1:SEQ], ALU.mult, ALU.add)
                            dve.drain()
                            dve.scalar_tensor_tensor(t[:, 2:SEQ], banks[r][:, 0:SEQ - 2], cols[:, bass.ds(c, 1)],
                                                     t[:, 2:SEQ], ALU.mult, ALU.add).then_inc(conv_done, 1)
                            dve.wait_ge(conv_done, layer * 2 * FT + i * 4 + (half * 2 + (2 - part)))
                        dve.sem_inc(tile_read[name], 2)
                        n = layer * FT + i * 2 + (half + 1)
                        dve.wait_ge(gelu_done, n)
                        dve.tensor_tensor(tmp[:, half * 2, :], tmp[:, half * 2, :], tmp[:, half * 2 + 1, :],
                                          ALU.mult).then_inc(h_ready, 1)
                        dve.wait_ge(h_hi_ready, n)
                        lo = h_lo[:, bass.ds(i * 2 + half, 1), :].rearrange("p a n -> p (a n)")
                        hi = h_hi[:, bass.ds(i * 2 + half, 1), :].rearrange("p a n -> p (a n)")
                        dve.tensor_tensor(lo, tmp[:, half * 2, :], hi.bitcast(F32), ALU.subtract)\
                            .then_inc(h_lo_ready, 1)

            def embed(layer):
                for k in range(PLE_TILES):
                    dve.wait_ge(p_hi_ready, layer * 2 + k + 1)
                    dve.tensor_tensor(p_lo[:, k, :], p_in[:, k, :], p_hi[:, k, :].bitcast(F32),
                                      ALU.subtract).then_inc(p_lo_ready, 1)

            def gate(layer):
                last = layer == DEPTH - 1
                with dve.Fori(0, 2) as i:
                    for r in range(4):
                        m = i * 4 + r
                        xm = x[:, bass.ds(m, 1), :].rearrange("p a n -> p (a n)")
                        dve.wait_ge(gated, i * 4 + (layer * KT + r + 1))
                        dve.tensor_tensor(tmp[:, r, :], tmp[:, r, :],
                                          emb[:, bass.ds(m, 1), :].rearrange("p a n -> p (a n)"), ALU.mult)
                        dve.drain()
                        dve.tensor_tensor(xm, xm, tmp[:, r, :], ALU.add).then_inc(emb_added, 1)
                        dve.drain()
                        if not last:
                            for m in next_tiles(r):
                                dve.wait_ge(x_hi_ready, i * 4 + (x_round[0] * KT + m + 1))
                                dve.tensor_tensor(one(next_lo, i * 4 + m), one(x, i * 4 + m),
                                                  one(next_hi, i * 4 + m).bitcast(F32),
                                                  ALU.subtract).then_inc(x_lo_ready, 1)
                x_round[0] += not last

            def rest_of_layer(layer):
                residual_phase(f"out{layer}", 2 * layer, 4, 1)
                dve.sem_inc(tile_read[f"up{layer}"], 4)
                layer_norm(2 * layer, layer, "ln1_g")
                dve.sem_inc(tile_read[f"down{layer}"], 2)
                conv_ffn(layer)
                embed(layer)
                residual_phase(f"down{layer}", 2 * layer + 1, 2, 3)
                layer_norm(2 * layer + 1, layer, "ln2_g")
                gate(layer)

            dve.sem_inc(h_lo_ready, 2)
            dve.sem_inc(rg_x_read, 2)
            dve.sem_inc(emb_added, 4)
            for layer in range(DEPTH):
                dve.sem_inc(tile_read[f"out{layer}"], 4)
            rest_of_layer(0)


            def rg_convolve(i, half):
                c = (i * 2 + half) * (CONV_B + 1) + COLS["rg_conv"]
                dve.wait_ge(rg_first, i * 2 + (half + 1))
                for lag in range(1, CONV_B):
                    dve.scalar_tensor_tensor(conv_x[:, half, lag:SEQ], banks[half][:, 0:SEQ - lag],
                                             cols[:, bass.ds(c + (CONV_B - 1 - lag), 1)],
                                             conv_x[:, half, lag:SEQ], ALU.mult, ALU.add)
                    dve.drain()
                dve.sem_inc(rg_x_read, 1)
                dve.sem_inc(rg_conv, 1)

            def rg_input(i, half):
                dve.wait_ge(rg_sig, i * 2 + (half + 3))
                dve.tensor_tensor(gate_i[:, half, :], gate_i[:, half, :], conv_x[:, half, :], ALU.mult)

            def rg_scan(i, half):
                dve.wait_ge(rg_sqrt, i * 2 + (half + 1))
                dve.scalar_tensor_tensor(drive[:], decay[:, half, :], 1.0, half_t[:, half, :], ALU.add, ALU.mult)
                dve.drain()
                dve.tensor_tensor(drive[:], drive[:], gate_i[:, half, :], ALU.mult)
                dve.drain()
                dve.tensor_tensor_scan(state[:, half, :], decay[:, half, :], drive[:], 0.0, ALU.mult, ALU.add)
                dve.drain()

            def rg_output(i, half):
                dve.wait_ge(rg_gelu, i * 2 + (half + 1))
                dve.tensor_tensor(state[:, half, :], state[:, half, :], gelu_g[:, half, :],
                                  ALU.mult).then_inc(rg_y, 1)

            def rg_low(i, half):
                dve.wait_ge(mix_hi_ready, i * 2 + (half + 1 + KT))
                m = i * 2 + half
                dve.tensor_tensor(one(mix_lo, m), state[:, half, :], one(mix_hi, m).bitcast(F32),
                                  ALU.subtract).then_inc(mix_lo_ready, 1)

            with dve.Fori(0, KT // 2) as i:
                for step in (rg_convolve, rg_input, rg_scan, rg_output, rg_low):
                    for half in range(2):
                        step(i, half)
            rest_of_layer(1)

        @block.scalar
        def _(act):
            def norm_squares(n):
                act.wait_ge(shift_done, n + 1)
                act.copy(shift[:], banks[6][:]).then_inc(shift_ready, 1)
                for m in range(KT):
                    act.wait_ge(dist_ready, n * KT + m + 1)
                    act.activation(dist[:, m % 2, :], dist[:, m % 2, :], ACT.Square).then_inc(square_done, 1)

            def layer_norm(n, layer, b, beside=None):
                act.wait_ge(var_ready, n + 1)
                act.activation(norm_stat[:, QT:2 * QT], norm_stat[:, QT:2 * QT], ACT.Sqrt,
                               bias=LN_EPS).then_inc(dev_ready, 1)
                if beside is not None:
                    beside(-1)
                for m in range(KT):
                    c = COLS[b, layer] + m
                    act.wait_ge(scaled, n * KT + m + 1)
                    act.activation(x_hi[:, m, :], x[:, m, :], ACT.Identity, bias=cols[:, c:c + 1])
                    act.activation(x[:, m, :], x[:, m, :], ACT.Identity,
                                   bias=cols[:, c:c + 1]).then_inc(x_hi_ready, 1)
                    if beside is not None:
                        beside(m)

            act.dma_start(wf[:], w_forget).then_inc(fg_w_loaded, 16)
            act.dma_start(bf[:], b_forget).then_inc(fg_w_loaded, 16)
            for n in range(KT // 4, KT // 2):
                act.dma_start(x[:, 2 * n:2 * n + 2, :], xT[:, 2 * n:2 * n + 2, :]).then_inc(x_loaded[n], 16)
            act.dma_start(cols[:], columns).then_inc(cols_loaded, 16)
            for m in range(KT):
                if m % 2 == 0:
                    act.wait_ge(x_loaded[m // 2], 16)
                act.copy(x_hi[:, m, :], x[:, m, :]).then_inc(x_hi_ready, 1)

            act.wait_ge(fg_abs, 1)
            act.activation(fg[:, 1, :], fg[:, 1, :], ACT.Exp, scale=-1.0).then_inc(fg_exp, 1)
            act.wait_ge(fg_rows, 1)
            act.dma_start(c_dram, c_rows[:].bitcast(F32)).then_inc(fg_stored, 16)
            act.wait_ge(lam_abs, 1)
            act.activation(lam4[:, 1, :], lam4[:, 1, :], ACT.Exp, scale=-1.0).then_inc(lam_exp, 1)
            act.wait_ge(fg_stored, 16)
            act.wait_ge(cols_loaded, 16)

            def keys(j, scored):
                act.wait_ge(unit_used, phases["qkv"].done(j, 1))
                if scored:
                    act.wait_ge(s_done, j * 2)
                act.dma_start(k_a[HEAD_DIM:HEAD_DIM + 2, :, :].bitcast(F32),
                              c_dram.rearrange("(j h) s n -> j s h n", h=2)[bass.ds(j, 1), :, :, :]
                              .rearrange("a s h n -> (a s) h n")).then_inc(row_loaded, 16)
                for to in (k_a, k_b):
                    for h in range(2):
                        act.copy(to[0:HEAD_DIM, h, :], banks[1][h * HEAD_DIM:(h + 1) * HEAD_DIM, :])
                act.drain()
                act.sem_inc(kv_read, 1)

            def values(j, turned):
                act.wait_ge(unit_used, phases["qkv"].done(j, 2))
                if turned:
                    act.wait_ge(vt_done, j)
                act.copy(v_chan[:], banks[0][:]).then_inc(kv_read, 1)

            def token_values(j):
                act.wait_ge(vt_done, j + 1)
                act.copy(v_tok[:].rearrange("p t c -> p (t c)"), banks[7][:]).then_inc(vt_read, 1)

            def exponentials(j, h, weighed):
                if weighed:
                    act.wait_ge(pt_done, j * 6 - (3 - h * 3))
                for n, (t, (bank, c)) in enumerate(((3, (2, 0)), (2, (3, 0)), (0, (3, 384)), (1, (4, 0)))):
                    act.wait_ge(max_ready, j * 8 + (h * 4 + max(n + 1, 3 if n in (1, 2) else 0)))
                    a0, w = t * (t + 1) // 2 * P, (t + 1) * P
                    act.activation(probs[:, h, a0:a0 + w], banks[bank][:, c:c + w], ACT.Exp,
                                   bias=stat[:, h, t:t + 1], accum_out=stat[:, h, 4 + t:5 + t])
                    act.drain()
                    act.sem_inc(exp_ready, 1)

            def turned_probs(j, h, weighed):
                for step, (bank, a0, w) in enumerate(((5, 0, 512), (6, 512, 384), (5, 896, 384))):
                    act.wait_ge(pt_done, j * 6 + (h * 3 + step + 1))
                    if step == 0 and weighed:
                        act.wait_ge(pv_done, j * 2 + h)
                    act.copy(probs_t[:, a0:a0 + w], banks[bank][:, 0:w]).then_inc(pt_read, 1)

            def outputs(j):
                act.wait_ge(pv_done, j * 2 + 2)
                act.copy(mix_hi[:, bass.ds(j, 1), :].rearrange("p a n -> p (a n)"), banks[7][:])\
                    .then_inc(mix_hi_ready, 1)

            def attend(j, j_next, project_it, first):
                exponentials(j, 0, not first)
                token_values(j)
                exponentials(j, 1, not first)
                turned_probs(j, 0, not first)
                if project_it:
                    keys(j_next, True)
                turned_probs(j, 1, True)
                outputs(j)
                if project_it:
                    values(j_next, True)

            act.sem_inc(pt_read, 1)
            act.sem_inc(exp_ready, 1)
            keys(0, False)
            values(0, False)
            attend(0, 1, True, True)
            with act.Fori(2, PAIRS) as j:
                attend(j - 1, j, True, False)
            attend(PAIRS - 1, None, False, False)

            def conv_ffn(layer):
                name = f"up{layer}"
                base = COLS["conv", layer]
                with act.Fori(0, FT // 2) as i:
                    for half in range(2):
                        act.wait_ge(unit_used, phases[name].done(i, half * 2 + 1))
                        act.wait_ge(h_lo_ready, i * 2 + (layer * FT + half + 1))
                        for part in (1, 0):
                            r = half * 2 + part
                            c = (i * 4 + r) * (CONV_F + 1) + base
                            act.activation(tmp[:, r, :], banks[r][:], ACT.Identity, bias=cols[:, bass.ds(c + 3, 1)],
                                           scale=cols[:, bass.ds(c + 2, 1)]).then_inc(conv_first, 1)
                        act.wait_ge(conv_done, i * 4 + (layer * 2 * FT + half * 2 + 1))
                        act.activation(tmp[:, half * 2 + 1, :], tmp[:, half * 2 + 1, :],
                                       ACT.Gelu_apprx_tanh).then_inc(gelu_done, 1)
                        act.wait_ge(h_ready, i * 2 + (layer * FT + half + 1))
                        act.copy(h_hi[:, bass.ds(i * 2 + half, 1), :].rearrange("p a n -> p (a n)"),
                                 tmp[:, half * 2, :]).then_inc(h_hi_ready, 1)

            def embedding_input(layer):
                act.wait_ge(unit_used, phases[f"up{layer}"].done(2 * FT // 4 - 1, 3))
                act.wait_ge(h_lo_ready, layer * FT + 2 + FT)
                act.dma_start(p_in[:], pT[layer]).then_inc(p_loaded, 16)
                act.wait_ge(p_loaded, 16 * (layer + 1))
                for k in range(PLE_TILES):
                    act.copy(p_hi[:, k, :], p_in[:, k, :]).then_inc(p_hi_ready, 1)

            def embedding(layer, a, b):
                for m in range(a, b):
                    act.wait_ge(emb_done, layer * KT + m + 1)
                    act.copy(emb[:, m, :], banks[2 + m % 4][:]).then_inc(tile_read[f"ple{layer}"], 1)

            def gate(layer):
                name = f"gate{layer}"
                with act.Fori(0, 2) as i:
                    for r in range(4):
                        act.wait_ge(unit_used, phases[name].done(i, r))
                        act.wait_ge(emb_added, i * 4 + (layer * KT + r + 1))
                        act.activation(tmp[:, r, :], banks[r][:], ACT.Sigmoid,
                                       bias=cols[:, bass.ds(i * 4 + (COLS["gate_b", layer] + r), 1)])\
                            .then_inc(gated, 1)
                        act.drain()
                        act.sem_inc(tile_read[name], 1)
                        if layer < DEPTH - 1:
                            for m in next_tiles(r):
                                act.wait_ge(emb_added, i * 4 + (4 + layer * KT + m + 1))
                                act.copy(one(next_hi, i * 4 + m), one(x, i * 4 + m)).then_inc(x_hi_ready, 1)

            def rest_of_layer(layer):
                norm_squares(2 * layer)
                layer_norm(2 * layer, layer, "ln1_b")
                conv_ffn(layer)
                embedding_input(layer)
                norm_squares(2 * layer + 1)
                act.sem_inc(tile_read[f"gate{layer}"], 4)
                layer_norm(2 * layer + 1, layer, "ln2_b", 
                           lambda m: embedding(layer, EMB_READ[m + 1], EMB_READ[m + 2]))
                gate(layer)

            act.sem_inc(rg_sig, 2)
            act.sem_inc(rg_g_read, 2)
            rest_of_layer(0)

            act.wait_ge(lam_abs, 2)
            rg = phases["rg"]

            def col(c):
                return cols[:, c:c + 1] if isinstance(c, int) else cols[:, bass.ds(c, 1)]

            def rg_blocks(i, reused):
                if reused:
                    act.wait_ge(rg_y, i * 2)
                for half in range(2):
                    c = (i * 2 + half) * (CONV_B + 1) + COLS["rg_conv"]
                    act.wait_ge(unit_used, rg.done(i, half))
                    act.activation(conv_x[:, half, :], banks[half][:], ACT.Identity, bias=col(c + CONV_B),
                                   scale=col(c + (CONV_B - 1))).then_inc(rg_first, 1)
                for half in range(2):
                    m = i * 2 + half
                    act.wait_ge(rg_gates, m + 3)
                    act.activation(gate_r[:, half, :], banks[4 + half * 2][:], ACT.Sigmoid,
                                   bias=col(m + COLS["rg_ba"]))
                    act.activation(gate_i[:, half, :], banks[5 + half * 2][:], ACT.Sigmoid,
                                   bias=col(m + COLS["rg_bi"]))
                    act.drain()
                    act.sem_inc(rg_sig, 1)
                for half in range(2):
                    at = bass.ds(i * 2 + half, 1) if not isinstance(i, int) else slice(half, half + 1)
                    act.activation(decay[:, half, :], gate_r[:, half, :], ACT.Exp, scale=lam4[:, 0, at])
                    act.activation(half_t[:, half, :], gate_r[:, half, :], ACT.Tanh, scale=lam4[:, 5, at])
                act.drain()
                for half in range(2):
                    act.activation(half_t[:, half, :], half_t[:, half, :], ACT.Sqrt).then_inc(rg_sqrt, 1)
                for half in range(2):
                    act.wait_ge(unit_used, rg.done(i, 2 + half))
                    act.activation(gelu_g[:, half, :], banks[2 + half][:], ACT.Gelu_apprx_tanh).then_inc(rg_gelu, 1)
                    act.drain()
                    act.sem_inc(rg_g_read, 1)
                for half in range(2):
                    act.wait_ge(rg_y, i * 2 + (half + 1))
                    act.copy(one(mix_hi, i * 2 + half), state[:, half, :]).then_inc(mix_hi_ready, 1)

            rg_blocks(0, False)
            with act.Fori(1, rg.iters) as i:
                rg_blocks(i, True)
            rest_of_layer(1)


def _tiles(w):
    k, n = w.shape[0] // P, w.shape[1] // P
    return w.reshape(k, P, n, P).transpose(2, 1, 0, 3).reshape(n, P, k * P)


def _per_channel(v):
    return v.reshape(-1, P).T


def kernel(**inputs):
    import numpy as np
    import concourse.bacc as bacc
    from concourse.bass_utils import run_bass_kernel_spmd

    g = {k: np.asarray(v) for k, v in inputs.items()}
    w_in = g["a_w_in"][0]
    q, k, v = (_tiles(w_in[:, n * D_MODEL:(n + 1) * D_MODEL]) for n in range(3))
    square = [t for j in range(PAIRS) for t in (q[j], k[j], v[j])] + list(_tiles(g["a_w_out"][0]))

    def rest(layer):
        up = _tiles(g["f_w_up"][layer])
        out = [up[half * FT + j] for j in range(FT) for half in range(2)]
        ple = _tiles(g["ple_w"][layer])
        out += [np.concatenate([ple[4 * n + c] for c in range(4)], axis=1) for n in range(2)]
        return out + list(_tiles(g["ple_gate_w"][layer]))

    square += rest(0)
    rg = _tiles(g["b_w_in"][0])
    square += [rg[part * KT + 2 * i + half] for i in range(KT // 2) for part in range(2) for half in range(2)]
    square += list(_tiles(g["b_w_out"][0])) + rest(1)
    columns = []
    for layer in range(DEPTH):
        for name in ("ln1_g", "ln1_b", "ln2_g", "ln2_b", "ple_gate_b"):
            columns.append(_per_channel(g[name][layer]))
        taps = np.stack([*g["f_conv_w"][layer], g["f_conv_b"][layer]])
        taps = taps.reshape(CONV_F + 1, 2, FT, P).transpose(3, 2, 1, 0)
        columns.append(taps.reshape(P, -1))
    taps = np.stack([*g["b_conv_w"][0], g["b_conv_b"][0]]).reshape(CONV_B + 1, KT, P)
    columns.append(taps.transpose(2, 1, 0).reshape(P, -1))
    columns += [_per_channel(g[n][0].reshape(-1)) for n in ("b_b_a", "b_b_i", "b_lam")]

    arrays = {
        "xT": g["x"][0].T.reshape(KT, P, SEQ).transpose(1, 0, 2),
        "pT": g["p"][:, 0].transpose(0, 2, 1).reshape(DEPTH, 2, P, SEQ).transpose(0, 2, 1, 3),
        "w_square": np.stack(square),
        "w_down": np.concatenate([_tiles(g["f_w_down"][layer]) for layer in range(DEPTH)]),
        "w_forget": w_in[:, 3 * D_MODEL:].reshape(KT, P, HEADS).transpose(1, 0, 2),
        "b_forget": g["a_b_f"].reshape(HEADS, 1),
        "w_lru": np.concatenate([g["b_w_a"][0], g["b_w_i"][0]], axis=2),
        "columns": np.concatenate(columns, axis=1),
    }
    arrays = {n: np.ascontiguousarray(a) for n, a in arrays.items()}
    assert arrays["columns"].shape == (P, N_COLS)
    nc = bacc.Bacc("TRN2", target_bir_lowering=False, num_devices=1)
    ins = [nc.dram_tensor(n, a.shape, F32, kind="ExternalInput").ap() for n, a in arrays.items()]
    out = nc.dram_tensor("outT", (KT, P, SEQ), F32, kind="ExternalOutput").ap()
    hybrid_trunk_kernel(nc, *ins, out)
    r = run_bass_kernel_spmd(nc, [arrays], core_ids=[0])
    return np.ascontiguousarray(np.asarray(r.results[0]["outT"]).reshape(D_MODEL, SEQ).T)[None]
```
